# Optimizing a Trainium2 kernel written in Bass

```python
import math
import jax, jax.numpy as jnp
from jax import lax
import numpy as np

D_MODEL = 1024
BATCH = 1
SEQ = 256
DEPTH = 2

ATTN_WIDTH = D_MODEL // 2
RNN_WIDTH = D_MODEL - ATTN_WIDTH
DIFF_HEAD_DIM = 64
N_DIFF_HEADS = ATTN_WIDTH // (2 * DIFF_HEAD_DIM)
V_HEAD_DIM = 2 * DIFF_HEAD_DIM
ROT_DIM = DIFF_HEAD_DIM // 4
ROPE_THETA = 500000.0
LRU_BLOCK = 64
N_LRU_BLOCKS = RNN_WIDTH // LRU_BLOCK
CONV_WIDTH = 4
LRU_C = 8.0
D_FF = 4 * D_MODEL
PLE_DIM = 256
Q_BLOCK = 128
EPS = 1e-6
IN_WIDTH = 3 * ATTN_WIDTH + 2 * RNN_WIDTH


def rms_norm(x, g):
    xf = x.astype(jnp.float32)
    y = xf * lax.rsqrt(jnp.mean(xf * xf, axis=-1, keepdims=True) + EPS)
    return (y * g.astype(jnp.float32)).astype(x.dtype)

def partial_rope(x, positions):
    half = ROT_DIM // 2
    inv_freq = ROPE_THETA ** (-jnp.arange(half, dtype=jnp.float32) * 2.0 / ROT_DIM)
    ang = positions.astype(jnp.float32)[..., None] * inv_freq
    cos = jnp.cos(ang)[:, :, None, None, :]
    sin = jnp.sin(ang)[:, :, None, None, :]
    xr = x[..., :ROT_DIM].astype(jnp.float32)
    x1, x2 = xr[..., :half], xr[..., half:]
    rot = jnp.concatenate([x1 * cos - x2 * sin, x2 * cos + x1 * sin], axis=-1)
    return jnp.concatenate([rot.astype(x.dtype), x[..., ROT_DIM:]], axis=-1)

def diff_attention(q, k, v, lam):
    B, S = q.shape[0], q.shape[1]
    nb = S // Q_BLOCK
    scale = DIFF_HEAD_DIM ** -0.5
    qb = q.reshape(B, nb, Q_BLOCK, N_DIFF_HEADS, 2, DIFF_HEAD_DIM).transpose(1, 0, 2, 3, 4, 5)
    q_idx = jnp.arange(S).reshape(nb, Q_BLOCK)
    k_idx = jnp.arange(S)

    def block(args):
        q_blk, qi = args
        s = jnp.einsum('bqhcd,bkhcd->bhcqk', q_blk, k).astype(jnp.float32) * scale
        mask = qi[:, None] >= k_idx[None, :]
        s = jnp.where(mask, s, -jnp.inf)
        pr = jax.nn.softmax(s, axis=-1)
        attn = pr[:, :, 0] - lam * pr[:, :, 1]
        return jnp.einsum('bhqk,bkhe->bqhe', attn.astype(v.dtype), v)

    out = lax.map(block, (qb, q_idx))
    return out.transpose(1, 0, 2, 3, 4).reshape(B, S, N_DIFF_HEADS, V_HEAD_DIM)

def causal_depthwise_conv(x, w, b):
    y = lax.conv_general_dilated(
        x, w[:, None, :].astype(x.dtype), window_strides=(1,),
        padding=[(CONV_WIDTH - 1, 0)],
        dimension_numbers=('NWC', 'WIO', 'NWC'),
        feature_group_count=x.shape[-1])
    return y + b

def rg_lru(x, w_a, b_a, w_x, b_x, lam_param):
    B, S, _ = x.shape
    xb = x.reshape(B, S, N_LRU_BLOCKS, LRU_BLOCK)
    r = jax.nn.sigmoid((jnp.einsum('bsgi,gij->bsgj', xb, w_a).reshape(B, S, RNN_WIDTH) + b_a).astype(jnp.float32))
    i = jax.nn.sigmoid((jnp.einsum('bsgi,gij->bsgj', xb, w_x).reshape(B, S, RNN_WIDTH) + b_x).astype(jnp.float32))
    log_a = -LRU_C * r * jax.nn.softplus(-lam_param.astype(jnp.float32))
    a = jnp.exp(log_a)
    b = jnp.sqrt(-jnp.expm1(2.0 * log_a)) * (i * x.astype(jnp.float32))

    def combine(left, right):
        a_l, b_l = left
        a_r, b_r = right
        return a_l * a_r, a_r * b_l + b_r

    _, h = lax.associative_scan(combine, (a, b), axis=1)
    return h.astype(x.dtype)

def first_inputs(seed: int = 0) -> dict:
    key = jax.random.key(seed)
    ks = jax.random.split(key, 24)
    f32 = jnp.float32
    nrm = lambda k, shape, s: jax.random.normal(k, shape, f32) * s
    gain = lambda k, shape: 1.0 + 0.05 * jax.random.normal(k, shape, f32)
    a0 = jax.random.uniform(ks[15], (DEPTH, RNN_WIDTH), f32, 0.9, 0.999)
    s0 = a0 ** (1.0 / LRU_C)
    lru_lambda = jnp.log(s0) - jnp.log1p(-s0)
    positions = jnp.broadcast_to(jnp.arange(SEQ, dtype=jnp.int32)[None, :], (BATCH, SEQ))
    return {
        'x': nrm(ks[0], (BATCH, SEQ, D_MODEL), 1.0),
        'p': nrm(ks[1], (DEPTH, BATCH, SEQ, PLE_DIM), 1.0),
        'positions': positions,
        'w_in': nrm(ks[2], (DEPTH, D_MODEL, IN_WIDTH), D_MODEL ** -0.5),
        'w_out': nrm(ks[3], (DEPTH, D_MODEL, D_MODEL), D_MODEL ** -0.5),
        'g_mix': gain(ks[4], (DEPTH, D_MODEL)),
        'g_subln': gain(ks[5], (DEPTH, V_HEAD_DIM)),
        'lam_q': nrm(ks[6], (DEPTH, 2, DIFF_HEAD_DIM), 0.1),
        'lam_k': nrm(ks[7], (DEPTH, 2, DIFF_HEAD_DIM), 0.1),
        'conv_w': nrm(ks[8], (DEPTH, CONV_WIDTH, RNN_WIDTH), CONV_WIDTH ** -0.5),
        'conv_b': nrm(ks[9], (DEPTH, RNN_WIDTH), 0.01),
        'w_gate_a': nrm(ks[10], (DEPTH, N_LRU_BLOCKS, LRU_BLOCK, LRU_BLOCK), LRU_BLOCK ** -0.5),
        'b_gate_a': nrm(ks[11], (DEPTH, RNN_WIDTH), 0.01),
        'w_gate_x': nrm(ks[12], (DEPTH, N_LRU_BLOCKS, LRU_BLOCK, LRU_BLOCK), LRU_BLOCK ** -0.5),
        'b_gate_x': nrm(ks[13], (DEPTH, RNN_WIDTH), 0.01),
        'lru_lambda': lru_lambda,
        'g_mlp': gain(ks[14], (DEPTH, D_MODEL)),
        'w_mlp_in': nrm(ks[16], (DEPTH, D_MODEL, D_FF), D_MODEL ** -0.5),
        'w_mlp_out': nrm(ks[17], (DEPTH, D_FF, D_MODEL), D_FF ** -0.5),
        'g_ple': gain(ks[18], (DEPTH, D_MODEL)),
        'w_ple_gate': nrm(ks[19], (DEPTH, D_MODEL, D_MODEL), D_MODEL ** -0.5),
        'w_ple_proj': nrm(ks[20], (DEPTH, PLE_DIM, D_MODEL), PLE_DIM ** -0.5),
        'g_final': gain(ks[21], (D_MODEL,)),
    }

def first_block(x, p, positions, w_in, w_out, g_mix, g_subln, lam_q, lam_k, conv_w, conv_b,
              w_gate_a, b_gate_a, w_gate_x, b_gate_x, lru_lambda, g_mlp, w_mlp_in, w_mlp_out,
              g_ple, w_ple_gate, w_ple_proj, g_final):
    B, S, _ = x.shape
    h = x
    A, R = ATTN_WIDTH, RNN_WIDTH
    for l in range(DEPTH):
        hn = rms_norm(h, g_mix[l])
        proj = hn @ w_in[l]
        q, k, v, xr, gr = jnp.split(proj, [A, 2 * A, 3 * A, 3 * A + R], axis=-1)
        q = partial_rope(q.reshape(B, S, N_DIFF_HEADS, 2, DIFF_HEAD_DIM), positions)
        k = partial_rope(k.reshape(B, S, N_DIFF_HEADS, 2, DIFF_HEAD_DIM), positions)
        v = v.reshape(B, S, N_DIFF_HEADS, V_HEAD_DIM)
        lam_init = 0.8 - 0.6 * math.exp(-0.3 * l)
        dots = jnp.sum(lam_q[l].astype(jnp.float32) * lam_k[l].astype(jnp.float32), axis=-1)
        lam = jnp.exp(dots[0]) - jnp.exp(dots[1]) + lam_init
        o = diff_attention(q, k, v, lam)
        o = (rms_norm(o, g_subln[l]) * (1.0 - lam_init)).reshape(B, S, A)
        xc = causal_depthwise_conv(xr, conv_w[l], conv_b[l])
        y = rg_lru(xc, w_gate_a[l], b_gate_a[l], w_gate_x[l], b_gate_x[l], lru_lambda[l])
        y = y * jax.nn.gelu(gr)
        h = h + jnp.concatenate([o, y], axis=-1) @ w_out[l]
        hm = rms_norm(h, g_mlp[l])
        h = h + jnp.square(jax.nn.relu(hm @ w_mlp_in[l])) @ w_mlp_out[l]
        gate = jax.nn.sigmoid(rms_norm(h, g_ple[l]) @ w_ple_gate[l])
        h = h + gate * (p[l] @ w_ple_proj[l])
    return rms_norm(h, g_final)


DEPTH_2 = 4

N_MIXERS = 3
N_A = (DEPTH_2 + 2) // 3
N_B = (DEPTH_2 + 1) // 3
N_C = DEPTH_2 // 3

N_HEADS = 16
HEAD_DIM = D_MODEL // N_HEADS
D_FF_2 = ((8 * D_MODEL // 3 + 127) // 128) * 128
ROT_DIM_2 = HEAD_DIM // 4
NEG = -1e30

MOBA_BLOCK = 256
MOBA_TOPK = 3
MOBA_Q_CHUNK = 32

MLA_Q_RANK = 384
MLA_KV_RANK = 256
MLA_NOPE = 64
MLA_ROPE = 32
MLA_V = 64
MLA_IN = MLA_Q_RANK + MLA_KV_RANK + MLA_ROPE


def rms_norm_2(x, g):
    xf = x.astype(jnp.float32)
    y = xf * lax.rsqrt(jnp.mean(xf * xf, axis=-1, keepdims=True) + EPS)
    return (y * g.astype(jnp.float32)).astype(x.dtype)

def rotary(x, pos):
    r = x.shape[-1]
    inv = ROPE_THETA ** (-jnp.arange(0, r, 2, dtype=jnp.float32) / r)
    ang = pos.astype(jnp.float32)[:, None] * inv[None, :]
    cos, sin = jnp.cos(ang), jnp.sin(ang)
    xf = x.astype(jnp.float32)
    x1, x2 = xf[..., : r // 2], xf[..., r // 2:]
    return jnp.concatenate([x1 * cos - x2 * sin, x1 * sin + x2 * cos], axis=-1).astype(x.dtype)

def partial_rotary(x, pos):
    return jnp.concatenate([rotary(x[..., :ROT_DIM_2], pos), x[..., ROT_DIM_2:]], axis=-1)

def to_heads(t):
    b, s, _ = t.shape
    return t.reshape(b, s, N_HEADS, -1).transpose(0, 2, 1, 3)

def from_heads(t):
    b, h, s, d = t.shape
    return t.transpose(0, 2, 1, 3).reshape(b, s, h * d)

def merge_blocks(o):
    nb, b, h, q, d = o.shape
    return o.transpose(1, 2, 0, 3, 4).reshape(b, h, nb * q, d)

def swiglu(x, w_gate_up, w_down):
    g, u = jnp.split(x @ w_gate_up, 2, axis=-1)
    return (jax.nn.silu(g) * u) @ w_down

def stick_breaking_attention(x, w_qkv, w_o):
    b, s, _ = x.shape
    q, k, v = (to_heads(t) for t in jnp.split(x @ w_qkv, 3, axis=-1))
    scale = HEAD_DIM ** -0.5
    kpos = jnp.arange(s)

    def block(i):
        q0 = i * Q_BLOCK
        qb = lax.dynamic_slice_in_dim(q, q0, Q_BLOCK, axis=2)
        z = jnp.einsum('bhqd,bhkd->bhqk', qb, k).astype(jnp.float32) * scale
        qpos = q0 + jnp.arange(Q_BLOCK)
        past = kpos[None, :] < qpos[:, None]
        log_keep = jnp.where(past, -jax.nn.softplus(z), 0.0)
        tail = lax.cumsum(log_keep, axis=3, reverse=True) - log_keep
        w = jnp.where(past, jnp.exp(jax.nn.log_sigmoid(z) + tail), 0.0)
        return jnp.einsum('bhqk,bhkd->bhqd', w.astype(v.dtype), v)

    o = merge_blocks(lax.map(block, jnp.arange(s // Q_BLOCK)))
    return from_heads(o) @ w_o

def moba_attention(x, w_qkv, w_o):
    b, s, _ = x.shape
    pos = jnp.arange(s)
    q, k, v = (to_heads(t) for t in jnp.split(x @ w_qkv, 3, axis=-1))
    q, k = partial_rotary(q, pos), partial_rotary(k, pos)
    nb = -(-s // MOBA_BLOCK)
    s_pad = nb * MOBA_BLOCK
    pad = [(0, 0), (0, 0), (0, s_pad - s), (0, 0)]
    q, k, v = jnp.pad(q, pad), jnp.pad(k, pad), jnp.pad(v, pad)
    kb = k.reshape(b, N_HEADS, nb, MOBA_BLOCK, HEAD_DIM)
    vb = v.reshape(b, N_HEADS, nb, MOBA_BLOCK, HEAD_DIM)
    scale = HEAD_DIM ** -0.5

    k_mean = jnp.mean(kb.astype(jnp.float32), axis=3)
    gate = jnp.einsum('bhsd,bhnd->bhsn', q.astype(jnp.float32), k_mean)
    q_blk = jnp.arange(s_pad) // MOBA_BLOCK
    past_blk = jnp.arange(nb)[None, :] < q_blk[:, None]
    gate = jnp.where(past_blk, gate, NEG)
    topk = min(MOBA_TOPK, nb)
    _, sel = lax.top_k(gate, topk)
    sel_valid = sel < q_blk[:, None]

    bi = jnp.arange(b)[:, None, None, None]
    hi = jnp.arange(N_HEADS)[None, :, None, None]

    def chunk(c):
        q0 = c * MOBA_Q_CHUNK
        qc = lax.dynamic_slice_in_dim(q, q0, MOBA_Q_CHUNK, axis=2)
        idx = lax.dynamic_slice_in_dim(sel, q0, MOBA_Q_CHUNK, axis=2)
        valid = lax.dynamic_slice_in_dim(sel_valid, q0, MOBA_Q_CHUNK, axis=2)
        kg = kb[bi, hi, idx]
        vg = vb[bi, hi, idx]
        l_sel = jnp.einsum('bhqd,bhqjkd->bhqjk', qc, kg).astype(jnp.float32) * scale
        l_sel = jnp.where(valid[..., None], l_sel, NEG)
        l_sel = l_sel.reshape(b, N_HEADS, MOBA_Q_CHUNK, topk * MOBA_BLOCK)
        own = q0 // MOBA_BLOCK
        k_own = lax.dynamic_index_in_dim(kb, own, axis=2, keepdims=False)
        v_own = lax.dynamic_index_in_dim(vb, own, axis=2, keepdims=False)
        l_own = jnp.einsum('bhqd,bhkd->bhqk', qc, k_own).astype(jnp.float32) * scale
        cpos = q0 + jnp.arange(MOBA_Q_CHUNK)
        opos = own * MOBA_BLOCK + jnp.arange(MOBA_BLOCK)
        l_own = jnp.where(opos[None, :] <= cpos[:, None], l_own, NEG)
        p = jax.nn.softmax(jnp.concatenate([l_sel, l_own], axis=-1), axis=-1).astype(v.dtype)
        p_sel = p[..., : topk * MOBA_BLOCK].reshape(b, N_HEADS, MOBA_Q_CHUNK, topk, MOBA_BLOCK)
        p_own = p[..., topk * MOBA_BLOCK:]
        return (jnp.einsum('bhqjk,bhqjkd->bhqd', p_sel, vg)
                + jnp.einsum('bhqk,bhkd->bhqd', p_own, v_own))

    o = merge_blocks(lax.map(chunk, jnp.arange(s_pad // MOBA_Q_CHUNK)))[:, :, :s]
    return from_heads(o) @ w_o

def mla_attention(x, w_in, q_norm, w_uq, kv_norm, w_ukv, w_o):
    b, s, _ = x.shape
    pos = jnp.arange(s)
    cq, ckv, kr = jnp.split(x @ w_in, [MLA_Q_RANK, MLA_Q_RANK + MLA_KV_RANK], axis=-1)
    q = to_heads(rms_norm_2(cq, q_norm) @ w_uq)
    q_nope, q_rope = q[..., :MLA_NOPE], rotary(q[..., MLA_NOPE:], pos)
    kv = to_heads(rms_norm_2(ckv, kv_norm) @ w_ukv)
    k_nope, v = kv[..., :MLA_NOPE], kv[..., MLA_NOPE:]
    k_rope = rotary(kr, pos)
    scale = (MLA_NOPE + MLA_ROPE) ** -0.5
    kpos = jnp.arange(s)

    def block(i):
        q0 = i * Q_BLOCK
        qn = lax.dynamic_slice_in_dim(q_nope, q0, Q_BLOCK, axis=2)
        qr = lax.dynamic_slice_in_dim(q_rope, q0, Q_BLOCK, axis=2)
        logits = (jnp.einsum('bhqd,bhkd->bhqk', qn, k_nope)
                  + jnp.einsum('bhqr,bkr->bhqk', qr, k_rope)).astype(jnp.float32) * scale
        qpos = q0 + jnp.arange(Q_BLOCK)
        logits = jnp.where(kpos[None, :] <= qpos[:, None], logits, NEG)
        p = jax.nn.softmax(logits, axis=-1).astype(v.dtype)
        return jnp.einsum('bhqk,bhkd->bhqd', p, v)

    o = merge_blocks(lax.map(block, jnp.arange(s // Q_BLOCK)))
    return from_heads(o) @ w_o

def second_inputs(seed: int = 0) -> dict:
    key = jax.random.key(seed)
    ks = iter(jax.random.split(key, 32))

    def w(shape, fan_in):
        return jax.random.normal(next(ks), shape, jnp.float32) * (fan_in ** -0.5)

    def gain(shape):
        return 1.0 + 0.02 * jax.random.normal(next(ks), shape, jnp.float32)

    D = D_MODEL
    return {
        "x": jax.random.normal(next(ks), (BATCH, SEQ, D), jnp.float32),
        "norm_ffn1": gain((DEPTH_2, D)),
        "ffn1_w_gate_up": w((DEPTH_2, D, 2 * D_FF_2), D),
        "ffn1_w_down": w((DEPTH_2, D_FF_2, D), D_FF_2),
        "norm_mix": gain((DEPTH_2, D)),
        "norm_ffn2": gain((DEPTH_2, D)),
        "ffn2_w_gate_up": w((DEPTH_2, D, 2 * D_FF_2), D),
        "ffn2_w_down": w((DEPTH_2, D_FF_2, D), D_FF_2),
        "sb_w_qkv": w((N_A, D, 3 * D), D),
        "sb_w_o": w((N_A, D, D), D),
        "moba_w_qkv": w((N_B, D, 3 * D), D),
        "moba_w_o": w((N_B, D, D), D),
        "mla_w_in": w((N_C, D, MLA_IN), D),
        "mla_q_norm": gain((N_C, MLA_Q_RANK)),
        "mla_w_uq": w((N_C, MLA_Q_RANK, N_HEADS * (MLA_NOPE + MLA_ROPE)), MLA_Q_RANK),
        "mla_kv_norm": gain((N_C, MLA_KV_RANK)),
        "mla_w_ukv": w((N_C, MLA_KV_RANK, N_HEADS * (MLA_NOPE + MLA_V)), MLA_KV_RANK),
        "mla_w_o": w((N_C, N_HEADS * MLA_V, D), N_HEADS * MLA_V),
        "final_norm": gain((D,)),
    }

def second_block(x, norm_ffn1, ffn1_w_gate_up, ffn1_w_down, norm_mix, norm_ffn2,
              ffn2_w_gate_up, ffn2_w_down, sb_w_qkv, sb_w_o, moba_w_qkv, moba_w_o,
              mla_w_in, mla_q_norm, mla_w_uq, mla_kv_norm, mla_w_ukv, mla_w_o,
              final_norm):
    h = x
    for i in range(DEPTH_2):
        h = h + 0.5 * swiglu(rms_norm_2(h, norm_ffn1[i]), ffn1_w_gate_up[i], ffn1_w_down[i])
        hn = rms_norm_2(h, norm_mix[i])
        kind, j = i % N_MIXERS, i // N_MIXERS
        if kind == 0:
            mix = stick_breaking_attention(hn, sb_w_qkv[j], sb_w_o[j])
        elif kind == 1:
            mix = moba_attention(hn, moba_w_qkv[j], moba_w_o[j])
        else:
            mix = mla_attention(hn, mla_w_in[j], mla_q_norm[j], mla_w_uq[j],
                                mla_kv_norm[j], mla_w_ukv[j], mla_w_o[j])
        h = h + mix
        h = h + 0.5 * swiglu(rms_norm_2(h, norm_ffn2[i]), ffn2_w_gate_up[i], ffn2_w_down[i])
    return rms_norm_2(h, final_norm)


def setup_inputs(seed=0):
    out = dict(first_inputs(seed))
    for name, value in second_inputs(seed + 1).items():
        if name != "x":
            out[name + "_2"] = value
    return out


def reference(
    x, p, positions, w_in, w_out, g_mix, g_subln, lam_q, lam_k, conv_w, conv_b, w_gate_a,
    b_gate_a, w_gate_x, b_gate_x, lru_lambda, g_mlp, w_mlp_in, w_mlp_out, g_ple, w_ple_gate,
    w_ple_proj, g_final, norm_ffn1_2, ffn1_w_gate_up_2, ffn1_w_down_2, norm_mix_2, norm_ffn2_2,
    ffn2_w_gate_up_2, ffn2_w_down_2, sb_w_qkv_2, sb_w_o_2, moba_w_qkv_2, moba_w_o_2, mla_w_in_2,
    mla_q_norm_2, mla_w_uq_2, mla_kv_norm_2, mla_w_ukv_2, mla_w_o_2, final_norm_2,
):
    x = first_block(
        x, p, positions, w_in, w_out, g_mix, g_subln, lam_q, lam_k, conv_w, conv_b, w_gate_a,
        b_gate_a, w_gate_x, b_gate_x, lru_lambda, g_mlp, w_mlp_in, w_mlp_out, g_ple, w_ple_gate,
        w_ple_proj, g_final,
    )
    return second_block(
        x, norm_ffn1_2, ffn1_w_gate_up_2, ffn1_w_down_2, norm_mix_2, norm_ffn2_2,
        ffn2_w_gate_up_2, ffn2_w_down_2, sb_w_qkv_2, sb_w_o_2, moba_w_qkv_2, moba_w_o_2,
        mla_w_in_2, mla_q_norm_2, mla_w_uq_2, mla_kv_norm_2, mla_w_ukv_2, mla_w_o_2,
        final_norm_2,
    )


_drawn_inputs = setup_inputs


def setup_inputs(seed=0):
    import zlib

    import numpy as np

    out = dict(_drawn_inputs(seed))
    spreads = {}
    factors = {'lam_q': 3.231,
     'b_gate_a': 8.0,
     'b_gate_x': 8.0,
     'g_ple': 6.744,
     'norm_ffn1_2': 4.065,
     'norm_ffn2_2': 4.866,
     'mla_q_norm_2': 8.0,
     'mla_kv_norm_2': 8.0,
     'final_norm_2': 2.783}
    for name, (base, spread) in spreads.items():
        noise = np.random.default_rng([zlib.crc32(name.encode()), seed]).standard_normal(out[name].shape)
        drawn = base * np.exp(spread * noise) if base else spread * noise
        out[name] = __import__('jax').numpy.asarray(drawn.astype(out[name].dtype))
    for name, factor in factors.items():
        out[name] = (out[name] * factor).astype(out[name].dtype)
    return out
```

```python
import math
from contextlib import ExitStack

import numpy as np
import concourse.bass as bass
from concourse import mybir

P = 128
SEQ, D = 256, 1024
TT = SEQ // P
KT = D // P
CH = 2048
RAW, SPLIT = 6, 3
DEPTH_A, DEPTH_B = 2, 4
D_FF_A = 4 * D
D_FF_B = ((8 * D // 3 + 127) // 128) * 128
PAIRS_A = D_FF_A // SEQ
PAIRS_B = D_FF_B // SEQ
HEADS, HD = 16, 64
MLA_QR, MLA_KVR, MLA_ROPE = 384, 256, 32
MLA_HD = HD + MLA_ROPE
MLA_IN = MLA_QR + MLA_KVR + MLA_ROPE
MLA_Q_GROUPS = [6, 6, 4]
EPS = 1e-6
NEG = -1e30
THETA = 500000.0
MIXERS = ["stick", "moba", "mla", "stick"]
CAUSAL = P + SEQ

CHUNKS_MIX_A, CHUNKS_PLE = 14, 5
CHUNKS_MLP, CHUNKS_FFN = 2 * PAIRS_A, 3 * PAIRS_B
CHUNKS_MIX_B = {"stick": 16, "moba": 16, "mla": 12}
N_CHUNKS = (DEPTH_A * (CHUNKS_MIX_A + CHUNKS_MLP + CHUNKS_PLE)
            + DEPTH_B * 2 * CHUNKS_FFN + sum(CHUNKS_MIX_B[m] for m in MIXERS))
assert N_CHUNKS % RAW == 0
BRIDGE = 3 * DEPTH_A
N_NORMS = 3 * DEPTH_A + 1 + 3 * DEPTH_B + 1
MLA_GAIN = N_NORMS

C_ID, C_ROT, C_ROTL, C_TRI, C_ALL, C_STRICT, C_CAUSNEG, C_STRNEG = [i * P for i in range(8)]
C_COSM, C_SINM, C_COSL, C_SINL = [8 * P + i * SEQ for i in range(4)]
C_FREQ = 8 * P + 4 * SEQ
C_END = C_FREQ + 1
L_CONV, L_CONVB, L_BA, L_BX, L_LAM, L_END = 0, 16, 20, 24, 28, 32


class Signals:

    def __init__(self, known, take):
        self.known, self.take = known, take
        self.sems, self.count, self.marks = {}, {}, {}

    def sem(self, name):
        if name not in self.sems:
            self.sems[name] = self.take(name)
            self.count[name] = 0
        return self.sems[name]

    def sig(self, name, key, by=1):
        sem = self.sem(name)
        self.count[name] += by
        assert (name, key) not in self.marks, (name, key)
        self.marks[name, key] = self.count[name]
        return sem, by

    def when(self, name, key):
        return self.sem(name), 1 if self.known is None else self.known[name, key]


def phases():
    out, c, n = [], 0, 0
    for l in range(DEPTH_A):
        out.append(("mix_a", l, c, n)); c += CHUNKS_MIX_A; n += 1
        out.append(("mlp", l, c, n)); c += CHUNKS_MLP; n += 1
        out.append(("ple", l, c, n)); c += CHUNKS_PLE; n += 1
    out.append(("bridge", 0, c, n)); n += 1
    for i in range(DEPTH_B):
        out.append(("ffn", 2 * i, c, n)); c += CHUNKS_FFN; n += 1
        out.append((MIXERS[i], i, c, n)); c += CHUNKS_MIX_B[MIXERS[i]]; n += 1
        out.append(("ffn", 2 * i + 1, c, n)); c += CHUNKS_FFN; n += 1
    out.append(("end", 0, c, n))
    return out


def write(nc, known, stream, x, pT, positions, gains, g_subln, lam_qk, lru_cols, gates, consts, out):
    f32, f32r, bf16 = mybir.dt.float32, mybir.dt.float32r, mybir.dt.bfloat16
    ALU, ACT, AX = mybir.AluOpType, mybir.ActivationFunctionType, mybir.AxisListType
    PHASES = phases()

    ctx = ExitStack()
    with ctx:
        def sb(name, shape, dt=f32):
            return ctx.enter_context(nc.sbuf_tensor(name, shape, dt))

        S = Signals(known, lambda name: ctx.enter_context(nc.semaphore(name)))
        sig, when = S.sig, S.when

        raw = sb("raw", [P, RAW, CH])
        w_hi = sb("w_hi", [P, SPLIT, CH], f32r)
        w_lo = sb("w_lo", [P, SPLIT, CH], f32r)
        h = sb("h", [P, TT, D])
        xn = sb("xn", [P, TT, D])
        xT = sb("xT", [P, KT, 2, SEQ], f32r)
        cat = sb("cat", [P, KT, 2, SEQ], f32r)
        big = sb("big", [P, 10496])
        gain = sb("gain", [P, D])
        cst = sb("cst", [P, C_END])
        ropeA = sb("ropeA", [P, 2, SEQ])
        small = sb("small", [P, 256])
        lru_par = sb("lru_par", [P, DEPTH_A, L_END])
        gsub = sb("gsub", [P, DEPTH_A, P])
        bfc = sb("bfc", [P, 4, P], bf16)
        zero = sb("zero", [P, 512], bf16)
        acc = ctx.enter_context(nc.psum_tensor("acc", [P, 4, 512], f32))
        tb = ctx.enter_context(nc.psum_tensor("tb", [P, 4, 512], f32))

        ident, rot, rotl = cst[:, C_ID:C_ID + P], cst[:, C_ROT:C_ROT + P], cst[:, C_ROTL:C_ROTL + P]
        tri, every, strict = cst[:, C_TRI:C_TRI + P], cst[:, C_ALL:C_ALL + P], cst[:, C_STRICT:C_STRICT + P]
        ident_b, causal_b, strict_b = bfc[:, 0, :], bfc[:, 1, :], bfc[:, 2, :]

        def cut(at, *shape):
            n = int(np.prod(shape))
            v = big[:, at:at + n]
            if len(shape) == 2:
                return v.rearrange("p (a b) -> p a b", a=shape[0])
            if len(shape) == 3:
                return v.rearrange("p (a b c) -> p a b c", a=shape[0], b=shape[1])
            return v

        f_act, f_hid = cut(0, 512), cut(512, 512)
        hid = cat[:, 0:6, :, :].rearrange("p (s f) a t -> p s f a t", s=3)
        a_q, a_k = cut(0, 4, SEQ), cut(1024, 4, SEQ)
        a_v = cut(2048, TT, 512)
        a_gr, a_xc, a_r, a_i, a_a, a_th = [cut(3072 + 1024 * i, 4, SEQ) for i in range(6)]
        a_x = cut(9216, 4, SEQ + 3)
        a_bd = xn[:, 0, :].rearrange("p (m f) -> p m f", m=8)
        a_o = cut(4096, TT, 512)
        b_q, b_k, b_v = cut(0, KT, SEQ), cut(2048, KT, SEQ), cut(4096, TT, D)
        s_e, s_l, s_w = [cut(6144 + 768 * i, 2, CAUSAL) for i in range(3)]
        m_q, m_k, m_v = cut(0, HEADS, SEQ), cut(4096, HEADS, SEQ), cut(8192, TT, D)
        rot_a = cut(9216, 512)
        flat_xn = xn[:, :, :].rearrange("p a b -> p (a b)")
        probs = flat_xn[:, 0:4 * CAUSAL].rearrange("p (s c) -> p s c", s=4)
        att_T = flat_xn[:, 4 * CAUSAL:4 * CAUSAL + 512]
        probs3 = flat_xn[:, 0:3 * CAUSAL].rearrange("p (s c) -> p s c", s=3)
        pT_two = flat_xn[:, 3 * CAUSAL:5 * CAUSAL].rearrange("p (s c) -> p s c", s=2)
        ss, ms, rms, r0, r1, r2, rstd = [small[:, 2 * i:2 * i + 2] for i in range(7)]
        mx, nmx, sm, rs = [small[:, 16 + 32 * i:48 + 32 * i].rearrange("p (m t) -> p m t", t=2) for i in range(4)]
        lam = small[:, 144:146]
        sp8, sp8n = small[:, 146:154], small[:, 154:162]
        t8a, t8b = small[:, 162:170], small[:, 170:178]
        s8 = [small[:, 178 + 8 * i:186 + 8 * i] for i in range(6)]
        cf = small[:, 226:228]
        dots = small[:, 228:232]
        dexp = small[:, 232:236]

        def split_hi(act, c, j=0, i=0):
            k = c + j
            if isinstance(i, int) and k + RAW * i >= N_CHUNKS:
                return
            act.wait_ge(raw_full[k % RAW], 16 * (k // RAW + 1) + 16 * i)
            if k >= SPLIT:
                act.wait_ge(chunk_used, k - SPLIT + 1 + RAW * i)
            act.activation(w_hi[:, k % SPLIT, :], raw[:, k % RAW, :], ACT.Copy).then_inc(hi_done, 1)

        def split_lo(dve, c, j=0, i=0):
            k = c + j
            if isinstance(i, int) and k + RAW * i >= N_CHUNKS:
                return
            dve.wait_ge(hi_done, k + 1 + RAW * i)
            dve.tensor_tensor(w_lo[:, k % SPLIT, :], raw[:, k % RAW, :], w_hi[:, k % SPLIT, :],
                              ALU.subtract).then_inc(lo_done, 1)

        def used(eng, k, i=0):
            eng.wait_ge(chunk_used, k + 1 + RAW * i)

        def columns(pe, c, dst, tiles, kts, width, i=0, src=None, m=P, after=None):
            src = xT if src is None else src
            pe.wait_ge(lo_done, c + 1 + RAW * i)
            s = c % SPLIT
            for f in range(tiles):
                for kt in range(kts):
                    at = kt * width + f * m
                    hi, lo = w_hi[:, s, at:at + m], w_lo[:, s, at:at + m]
                    if after is not None and f == 0:
                        after(kt)
                    pe.matmul(dst(f), hi, src[:, kt, 0, :], start=kt == 0, stop=False)
                    pe.matmul(dst(f), hi, src[:, kt, 1, :], start=False, stop=False)
                    last = pe.matmul(dst(f), lo, src[:, kt, 0, :], start=False, stop=kt == kts - 1)
            last.then_inc(chunk_used, 1)

        def rows(pe, c, dst, src, kts, n, start, stop, i=0, view=None, tok_done=None, after=None, inc=True):
            pe.wait_ge(lo_done, c + 1 + RAW * i)
            s = c % SPLIT
            for t in range(TT):
                for nn in range(n):
                    for kt in range(kts):
                        a_hi = src(kt)[:, 0, t * P:(t + 1) * P]
                        a_lo = src(kt)[:, 1, t * P:(t + 1) * P]
                        if after is not None and t == 0 and nn == 0:
                            after(kt)
                        b_hi, b_lo = view(w_hi, s, kt, nn), view(w_lo, s, kt, nn)
                        pe.matmul(dst(t, nn), a_hi, b_hi, start=start and kt == 0, stop=False)
                        pe.matmul(dst(t, nn), a_lo, b_hi, start=False, stop=False)
                        last = pe.matmul(dst(t, nn), a_hi, b_lo, start=False, stop=stop and kt == kts - 1)
                if tok_done is not None and t == 0:
                    last.then_inc(*sig("first_tokens", tok_done))
            last.then_inc(chunk_used, 1)

        def wide(w, s, kt, n):
            return w[:, s, kt * D + n * 512:kt * D + n * 512 + 512]

        def half(w, s, kt, n):
            return w[:, s, kt * SEQ:(kt + 1) * SEQ]

        def acc_tn(t, n):
            return acc[:, 2 * t + n, :]

        def norm_act(act, n, c):
            for t in range(TT):
                act.wait_ge(*(when("normed", (BRIDGE, t)) if n == BRIDGE + 1 else when("h_new", (n, t))))
                act.activation(xn[:, t, :], h[:, t, :], ACT.Square, accum_out=ss[:, t:t + 1]).then_inc(*sig("sumsq", (n, t)))
            act.wait_ge(*when("meansq", n))
            act.activation(rms, ms, ACT.Sqrt).then_inc(*sig("root", n))
            if n in (BRIDGE, N_NORMS - 1):
                return
            for b in range(4):
                act.wait_ge(*when("transposed", (n, b)))
                act.activation(xT[:, 2 * b:2 * b + 2, 0, :], tb[:, b, :].rearrange("p (k t) -> p k t", k=2),
                               ACT.Copy).then_inc(*sig("x_hi", (n, b)))

        def newton(dve, root, mean, a, b, out_, key):
            dve.wait_ge(*when("root", key))
            dve.reciprocal(a, root).then_inc(*sig("own", (key, "rc")))
            dve.wait_ge(*when("own", (key, "rc")))
            dve.tensor_tensor(b, a, a, ALU.mult).then_inc(*sig("own", (key, "sq")))
            dve.wait_ge(*when("own", (key, "sq")))
            dve.tensor_tensor(b, b, mean, ALU.mult).then_inc(*sig("own", (key, "xm")))
            dve.wait_ge(*when("own", (key, "xm")))
            dve.tensor_scalar(b, b, -0.5, 1.5, ALU.mult, ALU.add).then_inc(*sig("own", (key, "nt")))
            dve.wait_ge(*when("own", (key, "nt")))
            dve.tensor_tensor(out_, b, a, ALU.mult).then_inc(*sig("own", (key, "rstd")))
            dve.wait_ge(*when("own", (key, "rstd")))

        def norm_dve(dve, n, c):
            for t in range(TT):
                dve.wait_ge(*when("sumsq", (n, t)))
            dve.tensor_scalar(ms, ss, 1.0 / D, EPS, ALU.mult, ALU.add).then_inc(*sig("meansq", n))
            newton(dve, rms, ms, r0, r1, rstd, n)
            dve.wait_ge(*when("gain_in", n))
            for t in range(TT):
                to = h if n == BRIDGE else xn
                dve.scalar_tensor_tensor(to[:, t, :], h[:, t, :], rstd[:, t:t + 1], gain[:, :],
                                         ALU.mult, ALU.mult).then_inc(*sig("normed", (n, t)))
            if n in (BRIDGE, N_NORMS - 1):
                return
            for b in range(4):
                dve.wait_ge(*when("x_hi", (n, b)))
                dve.tensor_tensor(xT[:, 2 * b:2 * b + 2, 1, :], tb[:, b, :].rearrange("p (k t) -> p k t", k=2),
                                  xT[:, 2 * b:2 * b + 2, 0, :], ALU.subtract).then_inc(*sig("x_lo", (n, b)))

        def norm_pe(pe, n, c):
            pe.wait_ge(*when("normed", (n, 0)))
            pe.wait_ge(*when("normed", (n, 1)))
            for b in range(4):
                for kk in range(2):
                    for t in range(TT):
                        last = pe.transpose(tb[:, b, kk * SEQ + t * P:kk * SEQ + (t + 1) * P],
                                            xn[:, t, (2 * b + kk) * P:(2 * b + kk + 1) * P], ident)
                last.then_inc(*sig("transposed", (n, b)))

        def x_ready(pe, n):
            def after(kt):
                if kt % 2 == 0:
                    pe.wait_ge(*when("x_lo", (n, kt // 2)))
            return after

        def x_all(pe, n):
            pe.wait_ge(*when("x_lo", (n, 3)))

        def residual(dve, n, c_last, scale=1.0):
            for t in range(TT):
                if t == 0:
                    dve.wait_ge(*when("first_tokens", c_last))
                else:
                    used(dve, c_last)
                hv = h[:, t, :].rearrange("p (a b) -> p a b", a=2)
                dve.scalar_tensor_tensor(hv, acc[:, 2 * t:2 * t + 2, :], scale, hv,
                                         ALU.mult, ALU.add).then_inc(*sig("h_new", (n + 1, t)))

        def repeat(eng, turns, last_phase, body):
            apart = 1 if last_phase else 0
            with eng.Fori(0, turns - apart) as i:
                body(i)
            for i in range(turns - apart, turns):
                body(i)

        def zero_acc(pe, c):
            for b in range(4):
                pe.matmul(acc[:, b, :], zero[:, 0:P], zero[:, :], start=True, stop=False)

        def down(pe, c, k_slot, i=0, last=False):
            rows(pe, c, acc_tn, lambda kt: hid[:, k_slot, kt, :, :], 2, 2, False, last, i, wide,
                 tok_done=c if last else None)

        def up_a(pe, c, i=0, after=None):
            columns(pe, c, lambda f: tb[:, 0, f * SEQ:(f + 1) * SEQ], 2, KT, SEQ, i, after=after)

        def mlp_pe(pe, l, c, n):
            zero_acc(pe, c)
            up_a(pe, c, after=x_ready(pe, n))
            with pe.Fori(0, (PAIRS_A - 1) // 3) as i:
                for j in range(3):
                    pe.wait_ge(hid_t, HT[("mlp", l)] + 1 + j + 3 * i)
                    up_a(pe, c + 1 + 2 * j, i)
                    pe.wait_ge(hid_lo, HT[("mlp", l)] + 1 + j + 3 * i)
                    down(pe, c + 2 + 2 * j, j, i)
            pe.wait_ge(hid_lo, HT[("mlp", l)] + PAIRS_A)
            down(pe, c + CHUNKS_MLP - 1, (PAIRS_A - 1) % 3, last=True)

        def mlp_act(act, l, c, n):
            base = HT[("mlp", l)]

            def hidden(k, i=0):
                act.wait_ge(hid_t, base + 1 + k + 3 * i)
                s = k % 3
                act.activation(hid[:, s, :, 0, :], f_hid.rearrange("p (f t) -> p f t", f=2), ACT.Copy).then_inc(hid_hi, 1)

            hidden(0)
            split_hi(act, c, SPLIT)
            with act.Fori(0, (PAIRS_A - 1) // 3) as i:
                for j in range(3):
                    hidden(j + 1, i)
                    split_hi(act, c, 1 + 2 * j + SPLIT, i)
                    split_hi(act, c, 2 + 2 * j + SPLIT, i)
            split_hi(act, c, CHUNKS_MLP - 1 + SPLIT)

        def mlp_dve(dve, l, c, n):
            base = HT[("mlp", l)]

            def hidden(k, j, i=0):
                used(dve, c + j, i)
                if k:
                    dve.wait_ge(hid_lo, base + k + 3 * i)
                dve.tensor_scalar(f_act, tb[:, 0, :], 0.0, None, ALU.max).then_inc(hid_u, 1)
                dve.wait_ge(hid_u, BU[("mlp", l)] + 1 + k + 3 * i)
                dve.tensor_tensor(f_hid, f_act, f_act, ALU.mult).then_inc(hid_t, 1)
                dve.wait_ge(hid_hi, base + 1 + k + 3 * i)
                dve.tensor_tensor(hid[:, k % 3, :, 1, :], f_hid.rearrange("p (f t) -> p f t", f=2),
                                  hid[:, k % 3, :, 0, :], ALU.subtract).then_inc(hid_lo, 1)

            hidden(0, 0)
            split_lo(dve, c, SPLIT)
            with dve.Fori(0, (PAIRS_A - 1) // 3) as i:
                for j in range(3):
                    hidden(j + 1, 1 + 2 * j, i)
                    split_lo(dve, c, 1 + 2 * j + SPLIT, i)
                    split_lo(dve, c, 2 + 2 * j + SPLIT, i)
            split_lo(dve, c, CHUNKS_MLP - 1 + SPLIT)
            residual(dve, n, c + CHUNKS_MLP - 1)

        def up_b(pe, c, bank, i=0, after=None):
            columns(pe, c, lambda f: tb[:, bank, f * SEQ:(f + 1) * SEQ], 2, KT, SEQ, i, after=after)

        def ffn_pe(pe, f, c, n):
            base = HT[("ffn", f)]
            zero_acc(pe, c)
            up_b(pe, c, 0, after=x_ready(pe, n))
            up_b(pe, c + 1, 1)

            def turn(i):
                for j in range(2):
                    pe.wait_ge(hid_t, base + 1 + j + 2 * i)
                    up_b(pe, c + 2 + 3 * j, 0, i)
                    up_b(pe, c + 3 + 3 * j, 1, i)
                    pe.wait_ge(hid_lo, base + 1 + j + 2 * i)
                    down(pe, c + 4 + 3 * j, j, i)

            repeat(pe, (PAIRS_B - 1) // 2, f == 2 * DEPTH_B - 1, turn)
            pe.wait_ge(hid_lo, base + PAIRS_B)
            down(pe, c + CHUNKS_FFN - 1, (PAIRS_B - 1) % 2, last=True)

        def ffn_act(act, f, c, n):
            base, bu = HT[("ffn", f)], BU[("ffn", f)]

            def silu(k, j, i=0):
                used(act, c + j, i)
                act.activation(f_act, tb[:, 0, :], ACT.Silu).then_inc(hid_g, 1)

            def hidden(k, i=0):
                act.wait_ge(hid_t, base + 1 + k + 2 * i)
                act.activation(hid[:, k % 2, :, 0, :], f_hid.rearrange("p (f t) -> p f t", f=2), ACT.Copy).then_inc(hid_hi, 1)

            silu(0, 0)
            split_hi(act, c, SPLIT)
            hidden(0)
            split_hi(act, c, 1 + SPLIT)

            def turn(i):
                for j in range(2):
                    silu(j + 1, 2 + 3 * j, i)
                    split_hi(act, c, 2 + 3 * j + SPLIT, i)
                    hidden(j + 1, i)
                    split_hi(act, c, 3 + 3 * j + SPLIT, i)
                    split_hi(act, c, 4 + 3 * j + SPLIT, i)

            repeat(act, (PAIRS_B - 1) // 2, f == 2 * DEPTH_B - 1, turn)
            split_hi(act, c, CHUNKS_FFN - 1 + SPLIT)

        def ffn_dve(dve, f, c, n):
            base, bg = HT[("ffn", f)], BG[("ffn", f)]

            def hidden(k, j, i=0):
                used(dve, c + j, i)
                dve.wait_ge(hid_g, bg + 1 + k + 2 * i)
                if k:
                    dve.wait_ge(hid_lo, base + k + 2 * i)
                dve.tensor_tensor(f_hid, tb[:, 1, :], f_act, ALU.mult).then_inc(hid_t, 1)
                dve.wait_ge(hid_hi, base + 1 + k + 2 * i)
                dve.tensor_tensor(hid[:, k % 2, :, 1, :], f_hid.rearrange("p (f t) -> p f t", f=2),
                                  hid[:, k % 2, :, 0, :], ALU.subtract).then_inc(hid_lo, 1)

            split_lo(dve, c, SPLIT)
            hidden(0, 1)
            split_lo(dve, c, 1 + SPLIT)

            def turn(i):
                for j in range(2):
                    split_lo(dve, c, 2 + 3 * j + SPLIT, i)
                    hidden(j + 1, 3 + 3 * j, i)
                    split_lo(dve, c, 3 + 3 * j + SPLIT, i)
                    split_lo(dve, c, 4 + 3 * j + SPLIT, i)

            repeat(dve, (PAIRS_B - 1) // 2, f == 2 * DEPTH_B - 1, turn)
            split_lo(dve, c, CHUNKS_FFN - 1 + SPLIT)
            residual(dve, n, c + CHUNKS_FFN - 1, 0.5)

        HT, BU, BG = {}, {}, {}
        at = [0, 0, 0]
        for kind, l, c, n in PHASES:
            if kind in ("mlp", "ffn"):
                HT[kind, l], BU[kind, l], BG[kind, l] = at
                at[0] += PAIRS_A if kind == "mlp" else PAIRS_B
                at[1] += PAIRS_A if kind == "mlp" else 0
                at[2] += 0 if kind == "mlp" else PAIRS_B

        def ple_pe(pe, l, c, n):
            x_all(pe, n)
            pe.wait_ge(*when("p_lo", l))
            rows(pe, c, lambda t, nn: tb[:, 2 * t + nn, :], lambda kt: cat[:, kt, :, :], 2, 2, True, True, view=wide)
            for j in range(4):
                rows(pe, c + 1 + j, acc_tn, lambda kt: xT[:, 2 * j + kt, :, :], 2, 2, j == 0, j == 3,
                     view=wide, tok_done=c + 4 if j == 3 else None)

        def ple_act(act, l, c, n):
            act.wait_ge(*when("p_in", l))
            act.activation(cat[:, 0:2, 0, :], cut(0, 2, SEQ), ACT.Copy).then_inc(*sig("p_hi", l))
            for j in range(5):
                split_hi(act, c, j + SPLIT)
            for t in range(TT):
                if t == 0:
                    act.wait_ge(*when("first_tokens", c + 4))
                else:
                    used(act, c + 4)
                act.activation(xn[:, t, :].rearrange("p (a b) -> p a b", a=2), acc[:, 2 * t:2 * t + 2, :],
                               ACT.Sigmoid).then_inc(*sig("gate", (l, t)))

        def ple_dve(dve, l, c, n):
            dve.wait_ge(*when("p_hi", l))
            dve.tensor_tensor(cat[:, 0:2, 1, :], cut(0, 2, SEQ), cat[:, 0:2, 0, :], ALU.subtract).then_inc(*sig("p_lo", l))
            for j in range(5):
                split_lo(dve, c, j + SPLIT)
            for t in range(TT):
                dve.wait_ge(*when("gate", (l, t)))
                g = xn[:, t, :].rearrange("p (a b) -> p a b", a=2)
                dve.tensor_tensor(g, tb[:, 2 * t:2 * t + 2, :], g, ALU.mult).then_inc(*sig("own", ("ple", l, t)))
                dve.wait_ge(*when("own", ("ple", l, t)))
                dve.tensor_tensor(h[:, t, :], h[:, t, :], xn[:, t, :], ALU.add).then_inc(*sig("h_new", (n + 1, t)))

        def score_map(pe, bank, q, k, key, maps):
            b = tb[:, bank, :]
            pe.matmul(b[:, 0:P], q[:, 0:P], k[:, 0:P], start=True, stop=False)
            pe.matmul(b[:, 0:P], ident_b, causal_b, start=False, stop=True)
            pe.matmul(b[:, P:P + SEQ], q[:, P:SEQ], k, start=True, stop=True)
            pe.matmul(b[:, 2 * P:3 * P], ident_b, causal_b, start=False, stop=True, skip_group_check=True).then_inc(*sig("scores", key))

        def map_stats(dve, m, bank, key, scale):
            dve.wait_ge(*when("scores", key))
            dve.tensor_reduce(mx[:, m, 0:1], tb[:, bank, 0:P], AX.X, ALU.max)
            dve.tensor_reduce(mx[:, m, 1:2], tb[:, bank, P:CAUSAL], AX.X, ALU.max).then_inc(*sig("own", ("mx", key)))
            dve.wait_ge(*when("own", ("mx", key)))
            dve.tensor_scalar(nmx[:, m, :], mx[:, m, :], -scale, None, ALU.mult).then_inc(*sig("top", key))

        def map_exp(act, m, bank, dst, key, scale):
            act.wait_ge(*when("top", key))
            act.activation(dst[:, 0:P], tb[:, bank, 0:P], ACT.Exp, bias=nmx[:, m, 0:1], scale=scale,
                           accum_out=sm[:, m, 0:1])
            act.activation(dst[:, P:CAUSAL], tb[:, bank, P:CAUSAL], ACT.Exp, bias=nmx[:, m, 1:2], scale=scale,
                           accum_out=sm[:, m, 1:2]).then_inc(*sig("exps", key))

        def map_transpose(pe, bank, src, key):
            for j in range(3):
                last = pe.transpose(tb[:, bank, j * P:(j + 1) * P], src[:, j * P:(j + 1) * P], ident)
            last.then_inc(*sig("flipped", key))

        def heads_out(pe, hd, v, w, key):
            j, p0 = hd // 2, HD * (hd % 2)
            o = acc[p0:p0 + HD, j // 2, (j % 2) * SEQ:(j % 2 + 1) * SEQ]
            pe.matmul(o, v[:, 0, hd * HD:(hd + 1) * HD], w[:, 0:SEQ], start=True, stop=True)
            pe.matmul(o[:, P:SEQ], v[:, 1, hd * HD:(hd + 1) * HD], w[:, SEQ:CAUSAL], start=False,
                      stop=True, skip_group_check=True).then_inc(*sig("head_out", key))

        def cat_act(act, i):
            for b in range(4):
                act.wait_ge(*when("head_out", (i, 4 * b + 3)))
                act.activation(cat[:, 2 * b:2 * b + 2, 0, :], acc[:, b, :].rearrange("p (k t) -> p k t", k=2),
                               ACT.Copy).then_inc(*sig("cat_hi", (i, b)))

        def cat_dve(dve, i):
            for b in range(4):
                dve.wait_ge(*when("cat_hi", (i, b)))
                dve.tensor_tensor(cat[:, 2 * b:2 * b + 2, 1, :], acc[:, b, :].rearrange("p (k t) -> p k t", k=2),
                                  cat[:, 2 * b:2 * b + 2, 0, :], ALU.subtract).then_inc(*sig("cat_lo", (i, b)))

        def project_out(pe, i, c):
            pe.wait_ge(*when("cat_lo", (i, 3)))
            for j in range(4):
                rows(pe, c + j, acc_tn, lambda kt: cat[:, 2 * j + kt, :, :], 2, 2, j == 0, j == 3,
                     view=wide, tok_done=c + 3 if j == 3 else None)

        def softmax_pe(pe, i, c_out, q, k, v):
            for s in range(HEADS + 2):
                if s < HEADS:
                    if s >= 2:
                        pe.wait_ge(*when("exps", (i, s - 2)))
                    score_map(pe, s % 2, q(s), k(s), (i, s), None)
                if 1 <= s <= HEADS:
                    pe.wait_ge(*when("weights", (i, s - 1)))
                    if s >= 3:
                        pe.wait_ge(*when("flip_out", (i, s - 3)))
                    map_transpose(pe, 2 + (s - 1) % 2, probs3[:, (s - 1) % 3, :], (i, s - 1))
                if s >= 2:
                    pe.wait_ge(*when("flip_out", (i, s - 2)))
                    heads_out(pe, s - 2, v, pT_two[:, (s - 2) % 2, :], (i, s - 2))
            project_out(pe, i, c_out)

        def softmax_act(act, i, scale):
            for s in range(HEADS + 1):
                if s < HEADS:
                    if s >= 3:
                        act.wait_ge(*when("flipped", (i, s - 3)))
                    map_exp(act, s, s % 2, probs3[:, s % 3, :], (i, s), scale)
                if s >= 1:
                    act.wait_ge(*when("flipped", (i, s - 1)))
                    if s >= 3:
                        act.wait_ge(*when("head_out", (i, s - 3)))
                    act.activation(pT_two[:, (s - 1) % 2, :], tb[:, 2 + (s - 1) % 2, 0:CAUSAL],
                                   ACT.Copy).then_inc(*sig("flip_out", (i, s - 1)))
            cat_act(act, i)

        def softmax_dve(dve, i, scale):
            for s in range(HEADS + 1):
                if s < HEADS:
                    map_stats(dve, s, s % 2, (i, s), scale)
                if s >= 1:
                    m = s - 1
                    dve.wait_ge(*when("exps", (i, m)))
                    dve.reciprocal(rs[:, m, :], sm[:, m, :]).then_inc(*sig("own", ("rs", i, m)))
                    dve.wait_ge(*when("own", ("rs", i, m)))
                    pr = probs3[:, m % 3, :]
                    dve.tensor_scalar(pr[:, 0:P], pr[:, 0:P], rs[:, m, 0:1], None, ALU.mult)
                    dve.tensor_scalar(pr[:, P:CAUSAL], pr[:, P:CAUSAL], rs[:, m, 1:2], None,
                                      ALU.mult).then_inc(*sig("weights", (i, m)))
            cat_dve(dve, i)

        def qkv_pe(pe, kind, i, c, n):
            for j in range(4):
                rows(pe, c + j, lambda t, nn: acc[:, 2 * t + j // 2, (j % 2) * SEQ:(j % 2 + 1) * SEQ],
                     lambda kt: xT[:, kt, :, :], KT, 1, True, True, view=half,
                     after=x_ready(pe, n) if j == 0 else None)
            x_all(pe, n)
            for j in range(8):
                if j >= 4:
                    pe.wait_ge(*when("taken", (i, j - 4)))
                columns(pe, c + 4 + j, lambda f: tb[:, j % 4, f * SEQ:(f + 1) * SEQ], 2, KT, SEQ)
            if kind == "moba":
                pe.wait_ge(*when("v_out", (i, 1)))
                for j in range(8):
                    b = q_or_k(j)
                    pe.wait_ge(*when("taken", (i, j)))
                    if j >= 4:
                        pe.wait_ge(*when("turned", (i, j - 4)))
                    pe.matmul(acc[:, j % 4, :], rot, b, start=True, stop=True).then_inc(*sig("rotated", (i, j)))

        def q_or_k(j):
            b = b_q if j < 4 else b_k
            return b[:, 2 * (j % 4):2 * (j % 4) + 2, :].rearrange("p a t -> p (a t)")

        def qkv_act(act, kind, i, c, n):
            for j in range(4):
                if j % 2 == 1:
                    used(act, c + j)
                    for t in range(TT):
                        last = act.activation(b_v[:, t, (j // 2) * 512:(j // 2 + 1) * 512], acc[:, 2 * t + j // 2, :], ACT.Copy)
                    last.then_inc(*sig("v_out", (i, j // 2)))
                split_hi(act, c, j + SPLIT)
            for j in range(8):
                used(act, c + 4 + j)
                act.activation(q_or_k(j), tb[:, j % 4, :], ACT.Copy).then_inc(*sig("taken", (i, j)))
                split_hi(act, c, 4 + j + SPLIT)

        def qkv_dve(dve, kind, i, c, n):
            for j in range(12):
                split_lo(dve, c, j + SPLIT)
            if kind == "moba":
                for j in range(8):
                    b = q_or_k(j).rearrange("p (a t) -> p a t", a=2)
                    cos = cst[:, C_COSM:C_COSM + SEQ].unsqueeze(1).to_broadcast([P, 2, SEQ])
                    sin = cst[:, C_SINM:C_SINM + SEQ].unsqueeze(1).to_broadcast([P, 2, SEQ])
                    r = rot_a.rearrange("p (a t) -> p a t", a=2)
                    dve.wait_ge(*when("rotated", (i, j)))
                    if j:
                        dve.wait_ge(*when("turned", (i, j - 1)))
                    dve.tensor_tensor(r, acc[:, j % 4, :].rearrange("p (a t) -> p a t", a=2), sin, ALU.mult)
                    dve.tensor_tensor(b, b, cos, ALU.mult).then_inc(*sig("own", ("turn", i, j)))
                    dve.wait_ge(*when("own", ("turn", i, j)))
                    dve.tensor_tensor(b, b, r, ALU.add).then_inc(*sig("turned", (i, j)))

        def of_head(buf):
            return lambda hd: buf[HD * (hd % 2):HD * (hd % 2 + 1), hd // 2, :]

        def stick_pe(pe, i, c, n):
            qkv_pe(pe, "stick", i, c, n)
            q, k = of_head(b_q), of_head(b_k)
            pe.wait_ge(*when("taken", (i, 7)))
            pe.wait_ge(*when("v_out", (i, 1)))
            for s in range(HEADS + 2):
                if s < HEADS:
                    if s >= 4:
                        pe.wait_ge(*when("sticks", (i, s - 4)))
                    z = tb[:, s % 4, :]
                    pe.matmul(z[:, 0:SEQ], k(s)[:, 0:P], q(s), start=True, stop=True)
                    pe.matmul(z[:, SEQ:CAUSAL], k(s)[:, P:SEQ], q(s)[:, P:SEQ], start=False, stop=True,
                              skip_group_check=True).then_inc(*sig("scores", (i, s)))
                if 1 <= s <= HEADS:
                    m = s - 1
                    z, L = tb[:, m % 4, :], s_l[:, m % 2, :]
                    pe.wait_ge(*when("keeps", (i, m)))
                    pe.matmul(z[:, 0:SEQ], tri, L[:, 0:SEQ], start=False, stop=True, skip_group_check=True)
                    pe.matmul(z[:, P:SEQ], every, L[:, SEQ:CAUSAL], start=False, stop=True, skip_group_check=True)
                    pe.matmul(z[:, SEQ:CAUSAL], tri, L[:, SEQ:CAUSAL], start=False, stop=True, skip_group_check=True)
                    pe.matmul(z[:, 0:P], ident_b, strict_b, start=False, stop=True, skip_group_check=True)
                    pe.matmul(z[:, SEQ:CAUSAL], ident_b, strict_b, start=False, stop=True,
                              skip_group_check=True).then_inc(*sig("tails", (i, m)))
                if s >= 2:
                    pe.wait_ge(*when("sticks", (i, s - 2)))
                    heads_out(pe, s - 2, b_v, s_w[:, (s - 2) % 2, :], (i, s - 2))
            project_out(pe, i, c + 12)

        def stick_act(act, i, c, n):
            qkv_act(act, "stick", i, c, n)
            scale = HD ** -0.5
            for s in range(HEADS + 1):
                if s < HEADS:
                    e = s_e[:, s % 2, :]
                    act.wait_ge(*when("scores", (i, s)))
                    if s >= 2:
                        act.wait_ge(*when("keeps", (i, s - 2)))
                    act.activation(e, tb[:, s % 4, 0:CAUSAL], ACT.Abs, scale=scale).then_inc(*sig("own_act", ("a", i, s)))
                    act.wait_ge(*when("own_act", ("a", i, s)))
                    act.activation(e, e, ACT.Exp, scale=-1.0).then_inc(*sig("own_act", ("e", i, s)))
                    act.wait_ge(*when("own_act", ("e", i, s)))
                    act.activation(e, e, ACT.Ln, bias=1.0).then_inc(*sig("soft", (i, s)))
                if s >= 1:
                    m = s - 1
                    act.wait_ge(*when("tails", (i, m)))
                    if m >= 2:
                        act.wait_ge(*when("head_out", (i, m - 2)))
                    act.activation(s_w[:, m % 2, :], tb[:, m % 4, 0:CAUSAL], ACT.Exp,
                                   scale=scale).then_inc(*sig("sticks", (i, m)))
            cat_act(act, i)
            for j in range(12, 16):
                split_hi(act, c, j + SPLIT)

        def stick_dve(dve, i, c, n):
            qkv_dve(dve, "stick", i, c, n)
            scale = HD ** -0.5
            for s in range(HEADS):
                e, L = s_e[:, s % 2, :], s_l[:, s % 2, :]
                dve.wait_ge(*when("own_act", ("a", i, s)))
                if s >= 2:
                    dve.wait_ge(*when("tails", (i, s - 2)))
                dve.tensor_scalar(L, tb[:, s % 4, 0:CAUSAL], scale, 0.0, ALU.mult, ALU.max).then_inc(*sig("own", ("l", i, s)))
                dve.wait_ge(*when("own", ("l", i, s)))
                dve.wait_ge(*when("soft", (i, s)))
                dve.tensor_tensor(L, L, e, ALU.add).then_inc(*sig("own", ("m", i, s)))
                dve.wait_ge(*when("own", ("m", i, s)))
                dve.tensor_tensor(L[:, 0:P], L[:, 0:P], strict, ALU.mult)
                dve.tensor_tensor(L[:, SEQ:CAUSAL], L[:, SEQ:CAUSAL], strict, ALU.mult).then_inc(*sig("keeps", (i, s)))
            cat_dve(dve, i)
            for j in range(12, 16):
                split_lo(dve, c, j + SPLIT)
            residual(dve, n, c + 15)

        def moba_pe(pe, i, c, n):
            qkv_pe(pe, "moba", i, c, n)
            pe.wait_ge(*when("turned", (i, 7)))
            pe.wait_ge(*when("v_out", (i, 1)))
            softmax_pe(pe, i, c + 12, of_head(b_q), of_head(b_k), b_v)

        def moba_act(act, i, c, n):
            qkv_act(act, "moba", i, c, n)
            softmax_act(act, i, HD ** -0.5)
            for j in range(12, 16):
                split_hi(act, c, j + SPLIT)

        def moba_dve(dve, i, c, n):
            qkv_dve(dve, "moba", i, c, n)
            softmax_dve(dve, i, HD ** -0.5)
            for j in range(12, 16):
                split_lo(dve, c, j + SPLIT)
            residual(dve, n, c + 15)

        lat = xn[:, :, 0:MLA_IN]
        LAT_T = [(0, P), (P, P), (2 * P, P), (3 * P, P), (4 * P, P), (MLA_IN - MLA_HD, MLA_HD)]
        PAIRS = HEADS // 2
        q_of_pair = [(g, hd) for g, m in enumerate(MLA_Q_GROUPS) for hd in range(0, m, 2)]
        last_pair = {g: max(p for p, (gg, _) in enumerate(q_of_pair) if gg == g) for g in range(3)}
        kr_buf = cut(8192, SEQ)
        kr_rot = cut(8192 + SEQ, SEQ)

        def mla_pe(pe, i, c, n):
            for j in range(3):
                rows(pe, c + j, lambda t, nn: acc[:, (t if j < 2 else 2 + t), (j % 2) * SEQ:(j % 2 + 1) * SEQ],
                     lambda kt: xT[:, kt, :, :], KT, 1, True, True, view=half,
                     after=x_ready(pe, n) if j == 0 else None)
            pe.wait_ge(*when("lat_normed", i))
            for j, (at_, m) in enumerate(LAT_T):
                for t in range(TT):
                    last = pe.transpose(tb[0:m, j // 2, (j % 2) * SEQ + t * P:(j % 2) * SEQ + (t + 1) * P],
                                        lat[:, t, at_:at_ + m], ident)
                if j % 2 == 1:
                    last.then_inc(*sig("lat_T", (i, j // 2)))
            pe.wait_ge(*when("kr_in", i))
            pe.matmul(tb[0:MLA_HD, 3, 0:SEQ], rotl[0:MLA_HD, 0:MLA_HD], kr_buf[0:MLA_HD, :], start=True,
                      stop=True).then_inc(*sig("kr_rot", i))
            pe.wait_ge(*when("lat_lo", (i, 2)))
            pe.wait_ge(*when("kr_done", i))
            for p in range(PAIRS + 1):
                if p < PAIRS:
                    g, h0 = q_of_pair[p]
                    if p >= 2:
                        pe.wait_ge(*when("taken", (i, p - 2)))
                    pe.wait_ge(lo_done, c + 3 + g + 1)
                    s = (c + 3 + g) % SPLIT
                    width = MLA_Q_GROUPS[g] * MLA_HD
                    for u in range(2):
                        o = tb[0:MLA_HD, p % 2, u * SEQ:(u + 1) * SEQ]
                        for kt in range(3):
                            a = kt * width + (h0 + u) * MLA_HD
                            hi, lo = w_hi[:, s, a:a + MLA_HD], w_lo[:, s, a:a + MLA_HD]
                            pe.matmul(o, hi, xT[:, kt, 0, :], start=kt == 0, stop=False)
                            pe.matmul(o, hi, xT[:, kt, 1, :], start=False, stop=False)
                            last = pe.matmul(o, lo, xT[:, kt, 0, :], start=False, stop=kt == 2)
                    if p == last_pair[g]:
                        last.then_inc(chunk_used, 1)
                    else:
                        last.then_inc(*sig("pair_done", (i, p)))
                if p >= 1:
                    m = p - 1
                    pe.wait_ge(*when("taken", (i, m)))
                    if m >= 2:
                        pe.wait_ge(*when("turned", (i, m - 2)))
                    pe.matmul(acc[0:MLA_HD, m % 2, :], rotl[0:MLA_HD, 0:MLA_HD],
                              m_q[0:MLA_HD, 2 * m:2 * m + 2, :].rearrange("p a t -> p (a t)"),
                              start=True, stop=True).then_inc(*sig("rotated", (i, m)))
            for g in range(2):
                pe.wait_ge(lo_done, c + 6 + g + 1)
                s = (c + 6 + g) % SPLIT
                for p in range(4):
                    pp = PAIRS + 4 * g + p
                    pe.wait_ge(*when("taken", (i, pp - 2)))
                    for u in range(2):
                        o = tb[:, pp % 2, u * SEQ:(u + 1) * SEQ]
                        for kt in range(2):
                            a = kt * D + (2 * p + u) * P
                            hi, lo = w_hi[:, s, a:a + P], w_lo[:, s, a:a + P]
                            pe.matmul(o, hi, xT[:, 3 + kt, 0, :], start=kt == 0, stop=False)
                            pe.matmul(o, hi, xT[:, 3 + kt, 1, :], start=False, stop=False)
                            last = pe.matmul(o, lo, xT[:, 3 + kt, 0, :], start=False, stop=kt == 1)
                    last.then_inc(*sig("pair_done", (i, pp)))
                if g == 0:
                    pe.wait_ge(*when("turned", (i, PAIRS - 1)))

                def v_cols(w, s_, kt, nn):
                    return w[:, s_, kt * D:(kt + 1) * D].rearrange("p (h e) -> p h e", e=P)[:, :, HD:P]

                rows(pe, c + 6 + g, lambda t, nn: acc[:, 2 * t + g, :], lambda kt: xT[:, 3 + kt, :, :], 2, 1,
                     True, True, view=v_cols)
            pe.wait_ge(*when("taken", (i, 2 * PAIRS - 1)))
            pe.wait_ge(*when("v_out", (i, 1)))
            softmax_pe(pe, i, c + 8, lambda hd: m_q[0:MLA_HD, hd, :], lambda hd: m_k[0:MLA_HD, hd, :], m_v)

        def mla_act(act, i, c, n):
            for j in range(3):
                split_hi(act, c, j + SPLIT)
            act.wait_ge(*when("lat_ms", i))
            act.activation(s8[1][:, 0:4], s8[0][:, 0:4], ACT.Sqrt).then_inc(*sig("root", ("mla", i)))
            for b in range(3):
                act.wait_ge(*when("lat_T", (i, b)))
                if b < 2:
                    act.activation(xT[:, 2 * b:2 * b + 2, 0, :], tb[:, b, :].rearrange("p (k t) -> p k t", k=2),
                                   ACT.Copy).then_inc(*sig("lat_hi", (i, b)))
                else:
                    act.activation(kr_buf[0:MLA_HD, :], tb[0:MLA_HD, 2, SEQ:2 * SEQ], ACT.Copy).then_inc(*sig("kr_in", i))
                    act.activation(xT[:, 4, 0, :], tb[:, 2, 0:SEQ], ACT.Copy).then_inc(*sig("lat_hi", (i, 2)))
            for p in range(2 * PAIRS):
                if p < PAIRS and p == last_pair[q_of_pair[p][0]]:
                    used(act, c + 3 + q_of_pair[p][0])
                else:
                    act.wait_ge(*when("pair_done", (i, p)))
                b = m_q if p < PAIRS else m_k
                m = MLA_HD if p < PAIRS else HD
                hd = 2 * (p % PAIRS)
                act.activation(b[0:m, hd:hd + 2, :], tb[0:m, p % 2, :].rearrange("p (a t) -> p a t", a=2),
                               ACT.Copy).then_inc(*sig("taken", (i, p)))
                if p < PAIRS and p == last_pair[q_of_pair[p][0]]:
                    split_hi(act, c, 3 + q_of_pair[p][0] + SPLIT)
                if p in (PAIRS + 3, 2 * PAIRS - 1):
                    g = (p - PAIRS) // 4
                    used(act, c + 6 + g)
                    if g == 0:
                        act.wait_ge(*when("k_rope", i))
                    for t in range(TT):
                        last = act.activation(m_v[:, t, g * 512:(g + 1) * 512], acc[:, 2 * t + g, :], ACT.Copy)
                    last.then_inc(*sig("v_out", (i, g)))
                    split_hi(act, c, 6 + g + SPLIT)
            softmax_act(act, i, MLA_HD ** -0.5)
            for j in range(8, 12):
                split_hi(act, c, j + SPLIT)

        def mla_dve(dve, i, c, n):
            for j in range(3):
                used(dve, c + j)
                if j == 1:
                    dve.tensor_copy(lat[:, :, 0:512], acc[:, 0:2, :]).then_inc(*sig("own", ("lat0", i)))
                if j == 2:
                    dve.tensor_copy(lat[:, :, 512:MLA_IN], acc[:, 2:4, SEQ - (MLA_IN - 512):SEQ]).then_inc(*sig("own", ("lat1", i)))
                split_lo(dve, c, j + SPLIT)
            dve.wait_ge(*when("own", ("lat1", i)))
            junk = cut(0, 512)
            for k_, (a, b) in enumerate([(0, MLA_QR), (MLA_QR, MLA_QR + MLA_KVR)]):
                for t in range(TT):
                    sq = cut(1024 * (2 * k_ + t), b - a)
                    dve.tensor_tensor(sq, lat[:, t, a:b], lat[:, t, a:b], ALU.mult).then_inc(*sig("own", ("lsq", i, k_, t)))
                    dve.wait_ge(*when("own", ("lsq", i, k_, t)))
                    dve.tensor_reduce(s8[2][:, 2 * k_ + t:2 * k_ + t + 1], sq, AX.X, ALU.add).then_inc(*sig("own", ("lss", i, k_, t)))
            dve.wait_ge(*when("own", ("lss", i, 1, 1)))
            dve.tensor_scalar(s8[0][:, 0:2], s8[2][:, 0:2], 1.0 / MLA_QR, EPS, ALU.mult, ALU.add)
            dve.tensor_scalar(s8[0][:, 2:4], s8[2][:, 2:4], 1.0 / MLA_KVR, EPS, ALU.mult, ALU.add).then_inc(*sig("lat_ms", i))
            newton(dve, s8[1][:, 0:4], s8[0][:, 0:4], s8[3][:, 0:4], s8[4][:, 0:4], s8[5][:, 0:4], ("mla", i))
            dve.wait_ge(*when("gain_in", "mla"))
            for k_, (a, b) in enumerate([(0, MLA_QR), (MLA_QR, MLA_QR + MLA_KVR)]):
                for t in range(TT):
                    last = dve.scalar_tensor_tensor(lat[:, t, a:b], lat[:, t, a:b], s8[5][:, 2 * k_ + t:2 * k_ + t + 1],
                                                    gain[:, a:b], ALU.mult, ALU.mult)
            last.then_inc(*sig("lat_normed", i))
            for b in range(3):
                w = 2 if b < 2 else 1
                dve.wait_ge(*when("lat_hi", (i, b)))
                dve.tensor_tensor(xT[:, 2 * b:2 * b + w, 1, :], tb[:, b, 0:w * SEQ].rearrange("p (k t) -> p k t", k=w),
                                  xT[:, 2 * b:2 * b + w, 0, :], ALU.subtract).then_inc(*sig("lat_lo", (i, b)))
            R = slice(0, MLA_HD)
            cos, sin = cst[R, C_COSL:C_COSL + SEQ], cst[R, C_SINL:C_SINL + SEQ]
            dve.wait_ge(*when("kr_rot", i))
            dve.tensor_tensor(kr_rot[R, :], tb[R, 3, 0:SEQ], sin, ALU.mult)
            dve.tensor_tensor(kr_buf[R, :], kr_buf[R, :], cos, ALU.mult).then_inc(*sig("own", ("kr0", i)))
            dve.wait_ge(*when("own", ("kr0", i)))
            dve.tensor_tensor(kr_buf[R, :], kr_buf[R, :], kr_rot[R, :], ALU.add).then_inc(*sig("kr_done", i))
            dve.wait_ge(*when("kr_done", i))
            dve.tensor_copy(m_k[HD:MLA_HD, :, :], kr_buf[HD:MLA_HD, :].unsqueeze(1).to_broadcast([MLA_ROPE, HEADS, SEQ]))\
               .then_inc(*sig("k_rope", i))
            turn = xn[:, 1, 0:512].rearrange("p (a t) -> p a t", a=2)
            cos2, sin2 = cos.unsqueeze(1).to_broadcast([MLA_HD, 2, SEQ]), sin.unsqueeze(1).to_broadcast([MLA_HD, 2, SEQ])
            for p in range(PAIRS):
                g = q_of_pair[p][0]
                b = m_q[R, 2 * p:2 * p + 2, :]
                dve.wait_ge(*when("rotated", (i, p)))
                if p:
                    dve.wait_ge(*when("turned", (i, p - 1)))
                dve.tensor_tensor(turn[R, :, :], acc[R, p % 2, :].rearrange("p (a t) -> p a t", a=2), sin2, ALU.mult)
                dve.tensor_tensor(b, b, cos2, ALU.mult).then_inc(*sig("own", ("turn", i, p)))
                dve.wait_ge(*when("own", ("turn", i, p)))
                dve.tensor_tensor(b, b, turn[R, :, :], ALU.add).then_inc(*sig("turned", (i, p)))
                if p == last_pair[g]:
                    split_lo(dve, c, 3 + g + SPLIT)
            for g in range(2):
                split_lo(dve, c, 6 + g + SPLIT)
            softmax_dve(dve, i, MLA_HD ** -0.5)
            for j in range(8, 12):
                split_lo(dve, c, j + SPLIT)
            residual(dve, n, c + 11)

        A_DST = [a_x, a_x, a_gr, a_gr, a_q, a_q, a_k, a_k]

        def a_dst(j):
            d = A_DST[j]
            if j < 2:
                return d[:, 2 * j:2 * j + 2, 3:3 + SEQ]
            return d[:, 2 * (j % 2):2 * (j % 2) + 2, :]

        def mix_a_pe(pe, l, c, n):
            for j in range(8):
                if j >= 4:
                    pe.wait_ge(*when("a_taken", (l, j - 4)))
                columns(pe, c + j, lambda f: tb[:, j % 4, f * SEQ:(f + 1) * SEQ], 2, KT, SEQ,
                        after=x_ready(pe, n) if j == 0 else None)
                if j == 4:
                    pe.wait_ge(*when("conv", (l, 3)))
                    pe.wait_ge(*when("gates_in", l))
                    for g in range(8):
                        last = pe.matmul(acc[:, g // 2, (g % 2) * SEQ:(g % 2 + 1) * SEQ], a_bd[:, g, :],
                                         a_xc[:, g % 4, :], start=True, stop=True)
                    last.then_inc(*sig("gates", l))
            pe.wait_ge(*when("gate_sig", l))
            for j in range(2):
                rows(pe, c + 8 + j, lambda t, nn: acc[:, t, j * SEQ:(j + 1) * SEQ],
                     lambda kt: xT[:, kt, :, :], KT, 1, True, True, view=half)
            for j in range(4):
                pe.wait_ge(*when("a_taken", (l, 4 + j)))
                b = (a_q if j < 2 else a_k)[:, 2 * (j % 2):2 * (j % 2) + 2, :].rearrange("p a t -> p (a t)")
                pe.matmul(tb[:, j, :], rot, b, start=True, stop=True).then_inc(*sig("rotated", ("a", l, j)))
            pe.wait_ge(*when("turned", ("a", l, 3)))
            pe.wait_ge(*when("v_out", ("a", l)))
            for s in range(8 + 4):
                if s < 8:
                    if s >= 2:
                        pe.wait_ge(*when("exps", ("a", l, s - 2)))
                    hd, comp = s // 2, s % 2
                    r = slice(HD * comp, HD * comp + HD)
                    score_map(pe, s % 2, a_q[r, hd, :], a_k[r, hd, :], ("a", l, s), None)
                if s % 2 == 0 and 2 <= s <= 8:
                    hd = s // 2 - 1
                    pe.wait_ge(*when("weights", ("a", l, hd)))
                    map_transpose(pe, 2 + hd % 2, probs[:, 2 * (hd % 2) + 1, :], ("a", l, hd))
                if s % 2 == 0 and s >= 4:
                    hd = s // 2 - 2
                    if hd >= 4:
                        continue
                    pe.wait_ge(*when("flip_out", ("a", l, hd)))
                    w = att_T[:, 0:CAUSAL]
                    o = [acc[:, 2 + t, hd * P:(hd + 1) * P] for t in range(TT)]
                    v = [a_v[:, t, hd * P:(hd + 1) * P] for t in range(TT)]
                    pe.matmul(o[0], w[:, 0:P], v[0], start=True, stop=True)
                    pe.matmul(o[1], w[:, P:2 * P], v[0], start=True, stop=False)
                    pe.matmul(o[1], w[:, 2 * P:3 * P], v[1], start=False, stop=True).then_inc(*sig("head_out", ("a", l, hd)))
            pe.wait_ge(*when("o_normed", l))
            for j in range(4):
                for t in range(TT):
                    last = pe.transpose(tb[:, j // 2, (j % 2) * SEQ + t * P:(j % 2) * SEQ + (t + 1) * P],
                                        a_o[:, t, j * P:(j + 1) * P], ident)
            last.then_inc(*sig("o_T", l))
            pe.wait_ge(*when("cat_lo", ("a", l)))
            for j in range(4):
                rows(pe, c + 10 + j, acc_tn, lambda kt: cat[:, 2 * j + kt, :, :], 2, 2, j == 0, j == 3,
                     view=wide, tok_done=c + 13 if j == 3 else None)

        def mix_a_act(act, l, c, n):
            def take(j):
                used(act, c + j)
                act.activation(a_dst(j), tb[:, j % 4, :].rearrange("p (a t) -> p a t", a=2),
                               ACT.Copy).then_inc(*sig("a_taken", (l, j)))
                split_hi(act, c, j + SPLIT)

            for j in range(5):
                take(j)
            act.wait_ge(*when("gates", l))
            for t in range(4):
                act.activation(a_r[:, t, :], acc[:, t // 2, (t % 2) * SEQ:(t % 2 + 1) * SEQ], ACT.Sigmoid,
                               bias=lru_par[:, l, L_BA + t:L_BA + t + 1]).then_inc(*sig("own_act", ("r", l, t)))
            for t in range(4):
                last = act.activation(a_i[:, t, :], acc[:, 2 + t // 2, (t % 2) * SEQ:(t % 2 + 1) * SEQ], ACT.Sigmoid,
                                      bias=lru_par[:, l, L_BX + t:L_BX + t + 1])
            last.then_inc(*sig("gate_sig", l))
            for j in range(5, 8):
                take(j)
            act.wait_ge(*when("own_act", ("r", l, 3)))
            for t in range(4):
                act.activation(a_a[:, t, :], a_r[:, t, :], ACT.Exp, scale=sp8n[:, 4 * l + t:4 * l + t + 1])
                last = act.activation(a_th[:, t, :], a_r[:, t, :], ACT.Tanh, scale=sp8[:, 4 * l + t:4 * l + t + 1])
            last.then_inc(*sig("decay", l))
            for j in range(8, 10):
                split_hi(act, c, j + SPLIT)
            used(act, c + 9)
            act.activation(a_v[:, :, :], acc[:, 0:2, :], ACT.Copy).then_inc(*sig("v_out", ("a", l)))
            act.wait_ge(*when("lru_m", l))
            act.activation(a_th[:, :, :], a_th[:, :, :], ACT.Sqrt).then_inc(*sig("lru_root", l))
            act.activation(a_gr[:, :, :], a_gr[:, :, :], ACT.Gelu_apprx_tanh).then_inc(*sig("lru_gelu", l))
            act.wait_ge(*when("lru_y", l))
            act.activation(cat[:, 4:8, 0, :], a_gr[:, :, :], ACT.Copy).then_inc(*sig("y_hi", l))
            for s in range(9):
                if s < 8:
                    if s >= 4:
                        act.wait_ge(*when("flipped", ("a", l, s // 2 - 2)))
                    map_exp(act, s, s % 2, probs[:, s % 4, :], ("a", l, s), HD ** -0.5)
                if s % 2 == 0 and s >= 2:
                    hd = s // 2 - 1
                    act.wait_ge(*when("flipped", ("a", l, hd)))
                    if hd:
                        act.wait_ge(*when("head_out", ("a", l, hd - 1)))
                    act.activation(att_T[:, 0:CAUSAL], tb[:, 2 + hd % 2, 0:CAUSAL], ACT.Copy).then_inc(*sig("flip_out", ("a", l, hd)))
            act.wait_ge(*when("o_ms", l))
            act.activation(s8[1], s8[0], ACT.Sqrt).then_inc(*sig("root", ("a", l)))
            act.wait_ge(*when("o_T", l))
            act.activation(cat[:, 0:4, 0, :].rearrange("p (b k) t -> p b k t", b=2),
                           tb[:, 0:2, :].rearrange("p b (k t) -> p b k t", k=2), ACT.Copy).then_inc(*sig("cat_hi", ("a", l)))
            for j in range(10, 14):
                split_hi(act, c, j + SPLIT)

        def mix_a_dve(dve, l, c, n):
            for j in range(2):
                split_lo(dve, c, j + SPLIT)
            par = lru_par[:, l, :]
            for t in range(4):
                if t % 2 == 0:
                    dve.wait_ge(*when("a_taken", (l, t // 2)))
                for k_ in range(4):
                    src = a_x[:, t, k_:k_ + SEQ]
                    w = par[:, L_CONV + 4 * k_ + t:L_CONV + 4 * k_ + t + 1]
                    if k_ == 0:
                        ins = dve.tensor_scalar(a_xc[:, t, :], src, w, par[:, L_CONVB + t:L_CONVB + t + 1], ALU.mult, ALU.add)
                    else:
                        dve.wait_ge(*when("own", ("cv", l, t, k_ - 1)))
                        ins = dve.scalar_tensor_tensor(a_xc[:, t, :], src, w, a_xc[:, t, :], ALU.mult, ALU.add)
                    ins.then_inc(*(sig("conv", (l, t)) if k_ == 3 else sig("own", ("cv", l, t, k_))))
            for j in range(2, 8):
                split_lo(dve, c, j + SPLIT)
            dve.wait_ge(*when("gate_sig", l))
            dve.tensor_tensor(a_i[:, :, :], a_i[:, :, :], a_xc[:, :, :], ALU.mult)
            dve.wait_ge(*when("decay", l))
            dve.tensor_tensor(a_r[:, :, :], a_a[:, :, :], a_a[:, :, :], ALU.mult).then_inc(*sig("own", ("aa", l)))
            dve.wait_ge(*when("own", ("aa", l)))
            dve.scalar_tensor_tensor(a_th[:, :, :], a_r[:, :, :], 1.0, a_th[:, :, :], ALU.add, ALU.mult).then_inc(*sig("lru_m", l))
            for j in range(8, 10):
                split_lo(dve, c, j + SPLIT)
            cos = ropeA[:, 0, :].unsqueeze(1).to_broadcast([P, 2, SEQ])
            sin = ropeA[:, 1, :].unsqueeze(1).to_broadcast([P, 2, SEQ])
            for j in range(4):
                b = (a_q if j < 2 else a_k)[:, 2 * (j % 2):2 * (j % 2) + 2, :]
                r = a_r[:, 2 * (j % 2):2 * (j % 2) + 2, :]
                dve.wait_ge(*when("rotated", ("a", l, j)))
                if j == 0:
                    dve.wait_ge(*when("lru_m", l))
                if j >= 2:
                    dve.wait_ge(*when("turned", ("a", l, j - 2)))
                dve.tensor_tensor(r, tb[:, j, :].rearrange("p (a t) -> p a t", a=2), sin, ALU.mult)
                dve.tensor_tensor(b, b, cos, ALU.mult).then_inc(*sig("own", ("turn", "a", l, j)))
                dve.wait_ge(*when("own", ("turn", "a", l, j)))
                dve.tensor_tensor(b, b, r, ALU.add).then_inc(*sig("turned", ("a", l, j)))
            dve.wait_ge(*when("lru_root", l))
            dve.tensor_tensor(a_i[:, :, :], a_i[:, :, :], a_th[:, :, :], ALU.mult).then_inc(*sig("own", ("b", l)))
            dve.wait_ge(*when("own", ("b", l)))
            for t in range(4):
                last = dve.tensor_tensor_scan(a_xc[:, t, :], a_a[:, t, :], a_i[:, t, :], 0.0, ALU.mult, ALU.add)
            last.then_inc(*sig("own", ("scan", l)))
            dve.wait_ge(*when("own", ("scan", l)))
            dve.wait_ge(*when("lru_gelu", l))
            dve.tensor_tensor(a_gr[:, :, :], a_gr[:, :, :], a_xc[:, :, :], ALU.mult).then_inc(*sig("lru_y", l))
            dve.wait_ge(*when("y_hi", l))
            dve.tensor_tensor(cat[:, 4:8, 1, :], a_gr[:, :, :], cat[:, 4:8, 0, :], ALU.subtract).then_inc(*sig("own", ("y_lo", l)))
            for s in range(9):
                if s < 8:
                    map_stats(dve, s, s % 2, ("a", l, s), HD ** -0.5)
                if s >= 1:
                    m = s - 1
                    pr = probs[:, m % 4, :]
                    dve.wait_ge(*when("exps", ("a", l, m)))
                    dve.reciprocal(rs[:, m, :], sm[:, m, :]).then_inc(*sig("own", ("rs", "a", l, m)))
                    dve.wait_ge(*when("own", ("rs", "a", l, m)))
                    if m % 2 == 0:
                        dve.tensor_scalar(pr[:, 0:P], pr[:, 0:P], rs[:, m, 0:1], None, ALU.mult)
                        dve.tensor_scalar(pr[:, P:CAUSAL], pr[:, P:CAUSAL], rs[:, m, 1:2], None,
                                          ALU.mult).then_inc(*sig("own", ("p0", "a", l, m)))
                    else:
                        dve.tensor_scalar(cf, rs[:, m, :], lam[:, l:l + 1], -1.0, ALU.mult, ALU.mult).then_inc(*sig("own", ("cf", l, m)))
                        dve.wait_ge(*when("own", ("cf", l, m)))
                        dve.wait_ge(*when("own", ("p0", "a", l, m - 1)))
                        first = probs[:, (m - 1) % 4, :]
                        dve.scalar_tensor_tensor(pr[:, 0:P], pr[:, 0:P], cf[:, 0:1], first[:, 0:P], ALU.mult, ALU.add)
                        dve.scalar_tensor_tensor(pr[:, P:CAUSAL], pr[:, P:CAUSAL], cf[:, 1:2], first[:, P:CAUSAL],
                                                 ALU.mult, ALU.add).then_inc(*sig("weights", ("a", l, m // 2)))
                        dve.wait_ge(*when("weights", ("a", l, m // 2)))
            dve.wait_ge(*when("head_out", ("a", l, 3)))
            dve.tensor_copy(a_o[:, :, :], acc[:, 2:4, :]).then_inc(*sig("own", ("oc", l)))
            dve.wait_ge(*when("own", ("oc", l)))
            o2 = cut(5120, TT, 512)
            dve.tensor_tensor(o2, a_o[:, :, :], a_o[:, :, :], ALU.mult).then_inc(*sig("own", ("osq", l)))
            dve.wait_ge(*when("own", ("osq", l)))
            dve.tensor_reduce(s8[2], cut(5120, 8, P), AX.X, ALU.add).then_inc(*sig("own", ("oss", l)))
            dve.wait_ge(*when("own", ("oss", l)))
            dve.tensor_scalar(s8[0], s8[2], 1.0 / P, EPS, ALU.mult, ALU.add).then_inc(*sig("o_ms", l))
            newton(dve, s8[1], s8[0], s8[3], s8[4], s8[5], ("a", l))
            for t in range(TT):
                for hd in range(4):
                    o = a_o[:, t, hd * P:(hd + 1) * P]
                    last = dve.scalar_tensor_tensor(o, o, s8[5][:, 4 * t + hd:4 * t + hd + 1], gsub[:, l, :], ALU.mult, ALU.mult)
            last.then_inc(*sig("o_normed", l))
            dve.wait_ge(*when("cat_hi", ("a", l)))
            for b in range(2):
                last = dve.tensor_tensor(cat[:, 2 * b:2 * b + 2, 1, :], tb[:, b, :].rearrange("p (k t) -> p k t", k=2),
                                         cat[:, 2 * b:2 * b + 2, 0, :], ALU.subtract)
            last.then_inc(*sig("cat_lo", ("a", l)))
            for j in range(10, 14):
                split_lo(dve, c, j + SPLIT)
            residual(dve, n, c + 13)

        MIX = {"mix_a": (mix_a_pe, mix_a_act, mix_a_dve), "mlp": (mlp_pe, mlp_act, mlp_dve),
               "ple": (ple_pe, ple_act, ple_dve), "ffn": (ffn_pe, ffn_act, ffn_dve),
               "stick": (stick_pe, stick_act, stick_dve), "moba": (moba_pe, moba_act, moba_dve),
               "mla": (mla_pe, mla_act, mla_dve)}

        raw_full = [S.sem(f"raw_full{s}") for s in range(RAW)]
        hi_done, lo_done, chunk_used = S.sem("hi_done"), S.sem("lo_done"), S.sem("chunk_used")
        hid_t, hid_u, hid_g, hid_hi, hid_lo = [S.sem(n_) for n_ in ("hid_t", "hid_u", "hid_g", "hid_hi", "hid_lo")]
        block = ctx.enter_context(nc.Block())

        @block.sync
        def _(sp):
            def load(k, row, i=0):
                sp.dma_start(raw[:, k, :], stream[row, :, :]).then_inc(raw_full[k], 16)

            for k in range(RAW):
                load(k, k)
            with sp.Fori(0, N_CHUNKS // RAW - 1) as i:
                for k in range(RAW):
                    sp.wait_ge(lo_done, k + 1 + RAW * i)
                    load(k, i * RAW + (RAW + k), i)
            for t in range(TT):
                sp.wait_ge(*when("normed", (N_NORMS - 1, t)))
                sp.dma_start(out[t * P:(t + 1) * P, :], xn[:, t, :]).then_inc(*sig("stored", t, 16))
            sp.wait_ge(*when("stored", TT - 1))

        @block.gpsimd
        def _(pool):
            pool.dma_start(h[:, :, :], x.rearrange("(t p) d -> p t d", p=P)).then_inc(*sig("x_in", 0, 16))
            pool.dma_start(cst[:, :], consts).then_inc(*sig("const_in", 0, 16))
            pool.dma_start(lru_par[:, :, :], lru_cols).then_inc(*sig("start_in", 0, 16))
            pool.dma_start(ropeA[:, 1, :].bitcast(mybir.dt.int32), positions.partition_broadcast(P)).then_inc(*sig("start_in", 1, 16))
            pool.dma_start(gsub[:, :, :], g_subln.partition_broadcast(P)).then_inc(*sig("start_in", 2, 16))
            pool.dma_start(cut(0, 512), lam_qk.partition_broadcast(P)).then_inc(*sig("start_in", 3, 16))
            pool.memset(zero[:, :], 0.0).then_inc(*sig("zeroed", 0))
            pool.memset(a_x[:, :, 0:3], 0.0).then_inc(*sig("zeroed", "x"))
            for kind, l, c, n in PHASES:
                if n:
                    pool.wait_ge(*when("normed", (n - 1, 1)))
                pool.dma_start(gain[:, :], gains[n, :].partition_broadcast(P)).then_inc(*sig("gain_in", n, 16))
                if kind == "mix_a":
                    pool.wait_ge(*when("transposed", (n, 3)))
                    pool.dma_start(a_bd, gates[l, :, :]).then_inc(*sig("gates_in", l, 16))
                if kind == "ple":
                    pool.wait_ge(*when("h_new", (n, 1)))
                    pool.dma_start(cut(0, 2, SEQ), pT[l, :, :, :]).then_inc(*sig("p_in", l, 16))
                if kind == "mla":
                    pool.wait_ge(*when("normed", (n, 1)))
                    pool.dma_start(gain[:, 0:MLA_QR + MLA_KVR], gains[MLA_GAIN, 0:MLA_QR + MLA_KVR].partition_broadcast(P))\
                        .then_inc(*sig("gain_in", "mla", 16))
                    pool.wait_ge(*when("lat_normed", l))

        @block.tensor
        def _(pe):
            pe.wait_ge(*when("masks", 0))
            pe.wait_ge(*when("zeroed", 0))
            for kind, l, c, n in PHASES[:-1]:
                if kind == "bridge":
                    continue
                norm_pe(pe, n, c)
                MIX[kind][0](pe, l, c, n)

        @block.scalar
        def _(act):
            for k in range(SPLIT):
                split_hi(act, k)
            act.wait_ge(*when("dots", 0))
            act.activation(dexp, dots, ACT.Exp).then_inc(*sig("dexp", 0))
            act.wait_ge(*when("lam_abs", 0))
            act.activation(t8b, t8a, ACT.Exp, scale=-1.0).then_inc(*sig("own_act", "st0"))
            act.wait_ge(*when("own_act", "st0"))
            act.activation(t8b, t8b, ACT.Ln, bias=1.0).then_inc(*sig("lam_ln", 0))
            act.wait_ge(*when("angle", 0))
            act.activation(ropeA[:, 1, :], cut(1024, SEQ), ACT.Sin)
            act.activation(ropeA[:, 0, :], cut(1536, SEQ), ACT.Sin).then_inc(*sig("sines", 0))
            for kind, l, c, n in PHASES:
                norm_act(act, n, c)
                if kind not in ("bridge", "end"):
                    MIX[kind][1](act, l, c, n)

        @block.vector
        def _(dve):
            for k in range(SPLIT):
                split_lo(dve, k)
            steps = [0]

            def own(ins):
                steps[0] += 1
                ins.then_inc(*sig("own", ("start", steps[0])))
                dve.wait_ge(*when("own", ("start", steps[0])))

            dve.wait_ge(*when("const_in", 0))
            dve.tensor_copy(bfc[:, 0, :], ident)
            dve.tensor_copy(bfc[:, 1, :], cst[:, C_CAUSNEG:C_CAUSNEG + P])
            dve.tensor_copy(bfc[:, 2, :], cst[:, C_STRNEG:C_STRNEG + P]).then_inc(*sig("masks", 0))
            dve.wait_ge(*when("start_in", 3))
            prod = cut(512, 256)
            own(dve.tensor_tensor(prod, cut(0, 256), cut(256, 256), ALU.mult))
            dve.tensor_reduce(dots, prod.rearrange("p (a d) -> p a d", a=4), AX.X, ALU.add).then_inc(*sig("dots", 0))
            dve.scalar_tensor_tensor(t8a.rearrange("p (l t) -> p l t", l=2), lru_par[:, :, L_LAM:L_END], -1.0,
                                     lru_par[:, :, L_LAM:L_END], ALU.mult, ALU.max).then_inc(*sig("lam_abs", 0))
            dve.wait_ge(*when("dexp", 0))
            for l in range(DEPTH_A):
                init = 0.8 - 0.6 * math.exp(-0.3 * l)
                own(dve.tensor_tensor(lam[:, l:l + 1], dexp[:, 2 * l:2 * l + 1], dexp[:, 2 * l + 1:2 * l + 2], ALU.subtract))
                own(dve.tensor_scalar(lam[:, l:l + 1], lam[:, l:l + 1], init, None, ALU.add))
                own(dve.tensor_scalar(gsub[:, l, :], gsub[:, l, :], 1.0 - init, None, ALU.mult))
            own(dve.tensor_scalar(sp8.rearrange("p (l t) -> p l t", l=2), lru_par[:, :, L_LAM:L_END], -1.0, 0.0, ALU.mult, ALU.max))
            dve.wait_ge(*when("lam_ln", 0))
            own(dve.tensor_tensor(sp8, sp8, t8b, ALU.add))
            own(dve.tensor_scalar(sp8, sp8, 8.0, None, ALU.mult))
            own(dve.tensor_scalar(sp8n, sp8, -1.0, None, ALU.mult))
            ang, turns, angc, tmp = cut(1024, SEQ), cut(1280, SEQ), cut(1536, SEQ), cut(1792, SEQ)
            own(dve.tensor_copy(ang, ropeA[:, 1, :].bitcast(mybir.dt.int32)))
            own(dve.tensor_scalar(ang, ang, cst[:, C_FREQ:C_FREQ + 1], None, ALU.mult))
            magic = 1.5 * 2.0 ** 23
            own(dve.tensor_scalar(turns, ang, 1.0 / (2 * math.pi), magic, ALU.mult, ALU.add))
            own(dve.tensor_scalar(turns, turns, magic, None, ALU.subtract))
            p1 = 6.28125
            p2 = float(np.float32(round((2 * math.pi - p1) * 2 ** 20) / 2 ** 20))
            p3 = 2 * math.pi - p1 - p2
            for part in (p1, p2, p3):
                own(dve.scalar_tensor_tensor(ang, turns, -part, ang, ALU.mult, ALU.add))
            own(dve.tensor_scalar(ang, ang, 3.1415925, -3.1415925, ALU.min, ALU.max))
            own(dve.scalar_tensor_tensor(tmp, ang, -1.0, ang, ALU.mult, ALU.max))
            dve.tensor_scalar(angc, tmp, -1.0, math.pi / 2, ALU.mult, ALU.add).then_inc(*sig("angle", 0))
            dve.wait_ge(*when("sines", 0))
            dve.wait_ge(*when("x_in", 0))
            dve.nop().then_inc(*sig("h_new", (0, 0)))
            dve.nop().then_inc(*sig("h_new", (0, 1)))
            for kind, l, c, n in PHASES:
                norm_dve(dve, n, c)
                if kind == "mix_a":
                    dve.wait_ge(*when("zeroed", "x"))
                if kind not in ("bridge", "end"):
                    MIX[kind][2](dve, l, c, n)
    return S.marks


def write_program(new, declare):
    nc = new()
    known = write(nc, None, *declare(nc))
    nc = new()
    write(nc, known, *declare(nc))
    return nc


def constants():
    c = np.zeros((P, C_END), np.float32)
    k, m = np.arange(P)[:, None], np.arange(P)[None, :]
    c[:, C_ID:C_ID + P] = k == m
    for at, heads, first, half_ in ((C_ROT, (0, HD), 0, HD // 8), (C_ROTL, (0,), HD, MLA_ROPE // 2)):
        for h0 in heads:
            for j in range(half_):
                a = h0 + first + j
                c[a + half_, at + a] = -1.0
                c[a, at + a + half_] = 1.0
    c[:, C_TRI:C_TRI + P] = -8.0 * (k >= m)
    c[:, C_ALL:C_ALL + P] = -8.0
    c[:, C_STRICT:C_STRICT + P] = k < m
    c[:, C_CAUSNEG:C_CAUSNEG + P] = NEG * (m > k)
    c[:, C_STRNEG:C_STRNEG + P] = NEG * (k >= m)
    pos = np.arange(SEQ, dtype=np.float32)
    for cos_at, sin_at, r, firsts in ((C_COSM, C_SINM, HD // 4, (0, HD)), (C_COSL, C_SINL, MLA_ROPE, (HD,))):
        inv = np.float32(THETA) ** (-np.arange(0, r, 2, dtype=np.float32) / np.float32(r))
        ang = pos[None, :] * inv[:, None]
        c[:, cos_at:cos_at + SEQ] = 1.0
        for f in firsts:
            for half_ in range(2):
                rows_ = slice(f + half_ * (r // 2), f + (half_ + 1) * (r // 2))
                c[rows_, cos_at:cos_at + SEQ] = np.cos(ang)
                c[rows_, sin_at:sin_at + SEQ] = np.sin(ang)
                if r == HD // 4:
                    c[rows_, C_FREQ] = inv
    return c


def column_chunks(w, width=SEQ):
    kt = w.shape[0] // P
    v = w.reshape(kt, P, w.shape[1] // width, width)
    return list(v.transpose(2, 1, 0, 3).reshape(w.shape[1] // width, P, kt * width))


def row_chunks(w):
    return list(w.reshape(w.shape[0] // (2 * P), 2, P, D).transpose(0, 2, 1, 3).reshape(-1, P, 2 * D))


def lay_stream(a):
    out = []

    def woven(ups, downs):
        out.extend(u[0] for u in ups)
        for k in range(1, len(downs)):
            out.extend(u[k] for u in ups)
            out.append(downs[k - 1])
        out.append(downs[-1])

    for l in range(DEPTH_A):
        w = a["w_in"][l]
        q, k, v, xr, gr = (w[:, 512 * j:512 * (j + 1)] for j in range(5))
        for part in (xr, gr, q, k, v):
            out.extend(column_chunks(part))
        out.extend(row_chunks(a["w_out"][l]))
        woven([column_chunks(a["w_mlp_in"][l])], row_chunks(a["w_mlp_out"][l]))
        out.extend(row_chunks(a["w_ple_proj"][l]))
        out.extend(row_chunks(a["w_ple_gate"][l]))

    def swiglu(f, i):
        gu = a[f + "_w_gate_up_2"][i]
        woven([column_chunks(gu[:, :D_FF_B]), column_chunks(gu[:, D_FF_B:])], row_chunks(a[f + "_w_down_2"][i]))

    for i in range(DEPTH_B):
        swiglu("ffn1", i)
        kind = MIXERS[i]
        if kind == "mla":
            w = a["mla_w_in_2"][0]
            for at in (0, SEQ, MLA_IN - SEQ):
                out.extend(column_chunks(w[:, at:at + SEQ]))
            at = 0
            for heads in MLA_Q_GROUPS:
                n = heads * MLA_HD
                part = a["mla_w_uq_2"][0][:, at:at + n].reshape(3, P, n).transpose(1, 0, 2).reshape(P, 3 * n)
                out.append(np.pad(part, ((0, 0), (0, CH - 3 * n))))
                at += n
            for g in range(2):
                out.extend(row_chunks(a["mla_w_ukv_2"][0][:, g * D:(g + 1) * D]))
            out.extend(row_chunks(a["mla_w_o_2"][0]))
        else:
            w = a["sb_w_qkv_2"][i // 3] if kind == "stick" else a["moba_w_qkv_2"][0]
            o = a["sb_w_o_2"][i // 3] if kind == "stick" else a["moba_w_o_2"][0]
            for part in (w[:, 2 * D:], w[:, :D], w[:, D:2 * D]):
                out.extend(column_chunks(part))
            out.extend(row_chunks(o))
        swiglu("ffn2", i)
    assert len(out) == N_CHUNKS, len(out)
    return np.stack(out)


def lay_out(a):
    gains = []
    for l in range(DEPTH_A):
        gains += [a["g_mix"][l], a["g_mlp"][l], a["g_ple"][l]]
    gains.append(a["g_final"])
    for i in range(DEPTH_B):
        gains += [a["norm_ffn1_2"][i], a["norm_mix_2"][i], a["norm_ffn2_2"][i]]
    gains.append(a["final_norm_2"])
    mla = np.zeros((D,), np.float32)
    mla[:MLA_QR + MLA_KVR] = np.concatenate([a["mla_q_norm_2"][0], a["mla_kv_norm_2"][0]])
    gains.append(mla)
    lru, gates = [], []
    for l in range(DEPTH_A):
        r = [a["conv_w"][l].reshape(16, P)] + [a[n][l].reshape(4, P) for n in ("conv_b", "b_gate_a", "b_gate_x", "lru_lambda")]
        lru.append(np.concatenate(r))
        bd = np.zeros((P, 8, P), np.float32)
        for m, name in enumerate(("w_gate_a", "w_gate_x")):
            for g in range(8):
                o = HD * (g % 2)
                bd[o:o + HD, 4 * m + g // 2, o:o + HD] = a[name][l][g]
        gates.append(bd.reshape(P, 8 * P))
    p = a["p"][:, 0]
    return {
        "stream": lay_stream(a),
        "x": a["x"][0],
        "pT": np.ascontiguousarray(p.transpose(0, 2, 1).reshape(DEPTH_A, 2, P, SEQ).transpose(0, 2, 1, 3)),
        "positions": a["positions"][0],
        "gains": np.stack(gains),
        "g_subln": a["g_subln"],
        "lam_qk": np.concatenate([a["lam_q"].reshape(-1), a["lam_k"].reshape(-1)]),
        "lru_cols": np.ascontiguousarray(np.stack(lru).transpose(2, 0, 1)),
        "gates": np.stack(gates),
        "consts": constants(),
    }


def kernel(**inputs):
    import concourse.bacc as bacc
    from concourse.bass_utils import run_bass_kernel_spmd as run

    arrays = lay_out({k: np.asarray(v) for k, v in inputs.items()})

    def new():
        return bacc.Bacc("TRN2", target_bir_lowering=False, num_devices=1)

    def declare(nc):
        aps = [nc.dram_tensor("in_" + k, v.shape, mybir.dt.from_np(v.dtype), kind="ExternalInput").ap()
               for k, v in arrays.items()]
        return aps + [nc.dram_tensor("out", (SEQ, D), mybir.dt.float32, kind="ExternalOutput").ap()]

    nc = write_program(new, declare)
    r = run(nc, [{"in_" + k: v for k, v in arrays.items()}], core_ids=[0])
    return r.results[0]["out"].reshape(1, SEQ, D)
```

```python
import math
from contextlib import ExitStack

import numpy as np
import concourse.bass as bass
from concourse import mybir

P = 128
SEQ, D = 256, 1024
TT = SEQ // P
KT = D // P
CH = 2048
RAW, SPLIT = 6, 3
DEPTH_A, DEPTH_B = 2, 4
D_FF_A = 4 * D
D_FF_B = ((8 * D // 3 + 127) // 128) * 128
PAIRS_A = D_FF_A // SEQ
PAIRS_B = D_FF_B // SEQ
HEADS, HD = 16, 64
MLA_QR, MLA_KVR, MLA_ROPE = 384, 256, 32
MLA_HD = HD + MLA_ROPE
MLA_IN = MLA_QR + MLA_KVR + MLA_ROPE
MLA_Q_GROUPS = [6, 6, 4]
EPS = 1e-6
NEG = -1e30
THETA = 500000.0
MIXERS = ["stick", "moba", "mla", "stick"]
CAUSAL = P + SEQ

CHUNKS_MIX_A, CHUNKS_PLE = 14, 5
CHUNKS_MLP, CHUNKS_FFN = 2 * PAIRS_A, 3 * PAIRS_B
CHUNKS_MIX_B = {"stick": 16, "moba": 16, "mla": 12}
N_CHUNKS = (DEPTH_A * (CHUNKS_MIX_A + CHUNKS_MLP + CHUNKS_PLE)
            + DEPTH_B * 2 * CHUNKS_FFN + sum(CHUNKS_MIX_B[m] for m in MIXERS))
assert N_CHUNKS % RAW == 0
BRIDGE = 3 * DEPTH_A
N_NORMS = 3 * DEPTH_A + 1 + 3 * DEPTH_B + 1

C_ID, C_ROT, C_ROTL, C_TRI, C_ALL, C_STRICT, C_CAUSNEG, C_STRNEG = [i * P for i in range(8)]
C_COSM, C_SINM, C_COSL, C_SINL = [8 * P + i * SEQ for i in range(4)]
C_FREQ = 8 * P + 4 * SEQ
C_END = C_FREQ + 1
L_CONV, L_CONVB, L_BA, L_BX, L_LAM, L_END = 0, 16, 20, 24, 28, 32


class Signals:

    def __init__(self, known, take):
        self.known, self.take = known, take
        self.sems, self.count, self.marks = {}, {}, {}

    def sem(self, name):
        if name not in self.sems:
            self.sems[name] = self.take(name)
            self.count[name] = 0
        return self.sems[name]

    def sig(self, name, key, by=1):
        sem = self.sem(name)
        self.count[name] += by
        assert (name, key) not in self.marks, (name, key)
        self.marks[name, key] = self.count[name]
        return sem, by

    def when(self, name, key):
        return self.sem(name), 1 if self.known is None else self.known[name, key]


def phases():
    out, c, n = [], 0, 0
    for l in range(DEPTH_A):
        out.append(("mix_a", l, c, n)); c += CHUNKS_MIX_A; n += 1
        out.append(("mlp", l, c, n)); c += CHUNKS_MLP; n += 1
        out.append(("ple", l, c, n)); c += CHUNKS_PLE; n += 1
    out.append(("bridge", 0, c, n)); n += 1
    for i in range(DEPTH_B):
        out.append(("ffn", 2 * i, c, n)); c += CHUNKS_FFN; n += 1
        out.append((MIXERS[i], i, c, n)); c += CHUNKS_MIX_B[MIXERS[i]]; n += 1
        out.append(("ffn", 2 * i + 1, c, n)); c += CHUNKS_FFN; n += 1
    out.append(("end", 0, c, n))
    return out


def write(nc, known, stream, x, pT, positions, gains, gains_T, g_subln, lam_qk, lru_cols, gates, consts, out):
    f32, f32r, bf16 = mybir.dt.float32, mybir.dt.float32r, mybir.dt.bfloat16
    ALU, ACT, AX = mybir.AluOpType, mybir.ActivationFunctionType, mybir.AxisListType
    PHASES = phases()

    ctx = ExitStack()
    with ctx:
        def sb(name, shape, dt=f32):
            return ctx.enter_context(nc.sbuf_tensor(name, shape, dt))

        S = Signals(known, lambda name: ctx.enter_context(nc.semaphore(name)))
        sig, when = S.sig, S.when

        raw = sb("raw", [P, RAW, CH])
        w_hi = sb("w_hi", [P, SPLIT, CH], f32r)
        w_lo = sb("w_lo", [P, SPLIT, CH], f32r)
        h = sb("h", [P, TT, D])
        xn = sb("xn", [P, TT, D])
        xT = sb("xT", [P, KT, 2, SEQ], f32r)
        cat = sb("cat", [P, KT, 2, SEQ], f32r)
        big = sb("big", [P, 10256])
        gain = sb("gain", [P, D])
        gain_T = sb("gain_T", [P, N_NORMS, KT])
        rb_diag = sb("rb_diag", [P, 2 * SEQ])
        rb, diag = rb_diag[:, 0:SEQ], rb_diag[:, SEQ:2 * SEQ]
        cst = sb("cst", [P, C_END])
        ropeA = sb("ropeA", [P, 2, SEQ])
        small = sb("small", [P, 256])
        lru_par = sb("lru_par", [P, DEPTH_A, L_END])
        gsub = sb("gsub", [P, DEPTH_A, P])
        bfc = sb("bfc", [P, 4, P], bf16)
        zero = sb("zero", [P, 512], bf16)
        acc = ctx.enter_context(nc.psum_tensor("acc", [P, 4, 512], f32))
        tb = ctx.enter_context(nc.psum_tensor("tb", [P, 4, 512], f32))

        ident, rot, rotl = cst[:, C_ID:C_ID + P], cst[:, C_ROT:C_ROT + P], cst[:, C_ROTL:C_ROTL + P]
        tri, every, strict = cst[:, C_TRI:C_TRI + P], cst[:, C_ALL:C_ALL + P], cst[:, C_STRICT:C_STRICT + P]
        ident_b, causal_b, strict_b = bfc[:, 0, :], bfc[:, 1, :], bfc[:, 2, :]

        def cut(at, *shape):
            n = int(np.prod(shape))
            v = big[:, at:at + n]
            if len(shape) == 2:
                return v.rearrange("p (a b) -> p a b", a=shape[0])
            if len(shape) == 3:
                return v.rearrange("p (a b c) -> p a b c", a=shape[0], b=shape[1])
            return v

        f_act, f_hid, f_gate, f_up = [cut(512 * i, 512) for i in range(4)]

        def two(ap):
            return ap.rearrange("p (a t) -> p a t", a=2)

        hid = cat[:, 0:6, :, :].rearrange("p (s f) a t -> p s f a t", s=3)
        a_q, a_k = cut(0, 4, SEQ), cut(1024, 4, SEQ)
        a_v = cut(2048, TT, 512)
        a_gr, a_xc, a_r, a_i, a_a, a_th = [cut(3072 + 1024 * i, 4, SEQ) for i in range(6)]
        a_x = cut(9216, 4, SEQ + 3)
        a_bd = xn[:, 0, :].rearrange("p (m f) -> p m f", m=8)
        a_o = cut(6144, TT, 512)
        b_q, b_k, b_v = cut(0, KT, SEQ), cut(2048, KT, SEQ), cut(4096, TT, D)
        s_l, s_w = [[cut(6144 + 1536 * i + 768 * j, 2, CAUSAL) for j in range(2)] for i in range(2)]
        m_q, m_k, m_v = cut(0, HEADS, SEQ), cut(4096, HEADS, SEQ), cut(8192, TT, D)
        rot_a = cut(9216, 512)
        p_in = cut(4096, 2, SEQ)
        m_pT = [cut(6144 + CAUSAL * i, CAUSAL) for i in range(2)]
        flat_xn = xn[:, :, :].rearrange("p a b -> p (a b)")
        probs = flat_xn[:, 0:4 * CAUSAL].rearrange("p (s c) -> p s c", s=4)
        att_T = flat_xn[:, 4 * CAUSAL:4 * CAUSAL + 512]
        s_e = [flat_xn[:, 2 * CAUSAL * i:2 * CAUSAL * (i + 1)].rearrange("p (a b) -> p a b", a=2) for i in range(2)]
        l_pT = [att_T[:, 0:CAUSAL], rb_diag[:, 0:CAUSAL]]
        ss, ms, rms, r0, r1, r2, rstd = [small[:, 2 * i:2 * i + 2] for i in range(7)]
        mx, nmx, sm, rs = [small[:, 16 + 32 * i:48 + 32 * i].rearrange("p (m t) -> p m t", t=2) for i in range(4)]
        lam = small[:, 144:146]
        sp8, sp8n = small[:, 146:154], small[:, 154:162]
        t8a, t8b = small[:, 162:170], small[:, 170:178]
        s8 = [small[:, 178 + 8 * i:186 + 8 * i] for i in range(6)]
        cf = small[:, 226:228]
        dots = small[:, 228:232]
        dexp = small[:, 232:236]

        def split_hi(act, c, j=0, i=0):
            k = c + j
            if isinstance(i, int) and k + RAW * i >= N_CHUNKS:
                return
            act.wait_ge(raw_full[k % RAW], 16 * (k // RAW + 1) + 16 * i)
            if k >= SPLIT:
                act.wait_ge(chunk_used, k - SPLIT + 1 + RAW * i)
            act.activation(w_hi[:, k % SPLIT, :], raw[:, k % RAW, :], ACT.Copy).then_inc(hi_done, 1)

        def split_lo(dve, c, j=0, i=0):
            k = c + j
            if isinstance(i, int) and k + RAW * i >= N_CHUNKS:
                return
            dve.wait_ge(hi_done, k + 1 + RAW * i)
            dve.tensor_tensor(w_lo[:, k % SPLIT, :], raw[:, k % RAW, :], w_hi[:, k % SPLIT, :],
                              ALU.subtract).then_inc(lo_done, 1)

        def used(eng, k, i=0):
            eng.wait_ge(chunk_used, k + 1 + RAW * i)

        def columns_by_steps(pe, c, dst, tiles, kts, width, i=0, src=None, m=P, after=None):
            src = xT if src is None else src
            pe.wait_ge(lo_done, c + 1 + RAW * i)
            s = c % SPLIT
            order = [(f, kt) for f in range(tiles) for kt in range(kts)]
            if after is not None:
                order.sort(key=lambda step: step[1])
            for f, kt in order:
                at = kt * width + f * m
                hi, lo = w_hi[:, s, at:at + m], w_lo[:, s, at:at + m]
                if after is not None and f == 0:
                    after(kt)
                pe.matmul(dst(f), hi, src[:, kt, 0, :], start=kt == 0 and (after is None or f == 0), stop=False,
                          skip_group_check=after is not None)
                pe.matmul(dst(f), hi, src[:, kt, 1, :], start=False, stop=False, skip_group_check=after is not None)
                last = pe.matmul(dst(f), lo, src[:, kt, 0, :], start=False, stop=kt == kts - 1,
                                 skip_group_check=after is not None)
                if (f, kt) == (tiles - 1, kts - 1):
                    last.then_inc(chunk_used, 1)
                yield

        def columns(pe, *args, **kw):
            for _ in columns_by_steps(pe, *args, **kw):
                pass

        def rows(pe, c, dst, src, kts, n, start, stop, i=0, view=None, acc_done=None, after=None, before_last=None):
            pe.wait_ge(lo_done, c + 1 + RAW * i)
            s = c % SPLIT
            order = [(t, nn, kt) for t in range(TT) for nn in range(n) for kt in range(kts)]
            if after is not None:
                order.sort(key=lambda step: step[2])
            elif acc_done is not None:
                order.sort(key=lambda step: step[1])
            for t, nn, kt in order:
                a_hi = src(kt)[:, 0, t * P:(t + 1) * P]
                a_lo = src(kt)[:, 1, t * P:(t + 1) * P]
                if before_last is not None and (t, nn, kt) == (TT - 1, n - 1, 0):
                    before_last()
                if after is not None and (t, nn) == (0, 0):
                    after(kt)
                b_hi, b_lo = view(w_hi, s, kt, nn), view(w_lo, s, kt, nn)
                pe.matmul(dst(t, nn), a_hi, b_hi, start=start and kt == 0, stop=False)
                pe.matmul(dst(t, nn), a_lo, b_hi, start=False, stop=False)
                last = pe.matmul(dst(t, nn), a_hi, b_lo, start=False, stop=stop and kt == kts - 1)
                if acc_done is not None and kt == kts - 1 and (t, nn) != (1, 1):
                    last.then_inc(*sig("acc_done", (acc_done, t, nn)))
            last.then_inc(chunk_used, 1)

        def wide(w, s, kt, n):
            return w[:, s, kt * D + n * 512:kt * D + n * 512 + 512]

        def half(w, s, kt, n):
            return w[:, s, kt * SEQ:(kt + 1) * SEQ]

        def acc_tn(t, n):
            return acc[:, 2 * t + n, :]

        def h_ready(eng, n, t, half):
            if n == BRIDGE + 1:
                eng.wait_ge(*when("normed", (BRIDGE, t)))
            else:
                eng.wait_ge(*when("h_new", (n, t, half)))

        def flip(pe, n, t, half):
            h_ready(pe, n, t, half)
            for b in (2 * half, 2 * half + 1):
                for kk in range(2):
                    last = pe.transpose(tb[:, b, kk * SEQ + t * P:kk * SEQ + (t + 1) * P],
                                        h[:, t, (2 * b + kk) * P:(2 * b + kk + 1) * P], ident)
                if t:
                    last.then_inc(*sig("transposed", (n, b)))

        def flip_lower(pe, n):
            def before_last():
                h_ready(pe, n + 1, 1, 0)
                for t in range(TT):
                    flip(pe, n + 1, t, 0)
            return before_last if n + 1 not in (BRIDGE, N_NORMS - 1) else None

        def norm_pe(pe, n, last_kind):
            if last_kind in (None, "bridge"):
                for t in range(TT):
                    flip(pe, n, t, 0)
            if last_kind == "ple":
                h_ready(pe, n, 1, 1)
            flip(pe, n, 0, 1)
            if n == 0:
                flip(pe, n, 1, 1)

        def norm_act(act, n):
            for b in range(4):
                act.wait_ge(*when("transposed", (n, b)))
                for kt in (2 * b, 2 * b + 1):
                    last = act.activation(xT[:, kt, 0, :], tb[:, b, (kt % 2) * SEQ:(kt % 2 + 1) * SEQ], ACT.Copy,
                                          scale=gain_T[:, n, kt:kt + 1])
                last.then_inc(*sig("x_hi", (n, b)))

        def factor_act(act, n):
            for t in range(TT):
                h_ready(act, n, t, 0)
                h_ready(act, n, t, 1)
                act.activation(xn[:, t, :], h[:, t, :], ACT.Square, accum_out=ss[:, t:t + 1]).then_inc(*sig("sumsq", (n, t)))
            act.wait_ge(*when("meansq", n))
            act.activation(rms, ms, ACT.Sqrt).then_inc(*sig("root", n))

        def spread_act(act, n, kind):
            if kind not in ("ple", "bridge", "end"):
                act.wait_ge(*when("spread", n))
                act.activation(rb, tb[:, 3, 0:SEQ], ACT.Copy).then_inc(*sig("rb", n))

        def spread(pe, n):
            pe.wait_ge(*when("diag", n))
            pe.matmul(tb[:, 3, 0:SEQ], every, diag, start=True, stop=True).then_inc(*sig("spread", n))

        def newton(dve, root, mean, a, b, out_, key):
            dve.wait_ge(*when("root", key))
            dve.reciprocal(a, root).then_inc(*sig("own", (key, "rc")))
            dve.wait_ge(*when("own", (key, "rc")))
            dve.tensor_tensor(b, a, a, ALU.mult).then_inc(*sig("own", (key, "sq")))
            dve.wait_ge(*when("own", (key, "sq")))
            dve.tensor_tensor(b, b, mean, ALU.mult).then_inc(*sig("own", (key, "xm")))
            dve.wait_ge(*when("own", (key, "xm")))
            dve.tensor_scalar(b, b, -0.5, 1.5, ALU.mult, ALU.add).then_inc(*sig("own", (key, "nt")))
            dve.wait_ge(*when("own", (key, "nt")))
            dve.tensor_tensor(out_, b, a, ALU.mult).then_inc(*sig("own", (key, "rstd")))
            dve.wait_ge(*when("own", (key, "rstd")))

        def x_low(dve, n, b):
            dve.wait_ge(*when("x_hi", (n, b)))
            for kt in (2 * b, 2 * b + 1):
                last = dve.scalar_tensor_tensor(xT[:, kt, 1, :], tb[:, b, (kt % 2) * SEQ:(kt % 2 + 1) * SEQ],
                                                gain_T[:, n, kt:kt + 1], xT[:, kt, 0, :], ALU.mult, ALU.subtract)
            last.then_inc(*sig("x_lo", (n, b)))

        def norm_dve(dve, n, last_kind):
            for b in range(0 if last_kind in (None, "bridge") else 1, 4):
                x_low(dve, n, b)

        def factor_dve(dve, n, kind):
            for t in range(TT):
                dve.wait_ge(*when("sumsq", (n, t)))
            dve.tensor_scalar(ms, ss, 1.0 / D, EPS, ALU.mult, ALU.add).then_inc(*sig("meansq", n))
            newton(dve, rms, ms, r0, r1, rstd, n)
            if kind == "ple":
                dve.nop().then_inc(*sig("rstd", n))
            elif kind not in ("bridge", "end"):
                for t in range(TT):
                    last = dve.tensor_scalar(diag[:, t * P:(t + 1) * P], ident, rstd[:, t:t + 1], -0.125, ALU.mult, ALU.mult)
                last.then_inc(*sig("diag", n))
            else:
                dve.wait_ge(*when("gain_in", n))
                for t in range(TT):
                    to = h if kind == "bridge" else xn
                    dve.scalar_tensor_tensor(to[:, t, :], h[:, t, :], rstd[:, t:t + 1], gain[:, :],
                                             ALU.mult, ALU.mult).then_inc(*sig("normed", (n, t)))

        def by_rb(dve, dst, src, n, first):
            if first:
                dve.wait_ge(*when("rb", n))
            a = dst.shape[1]
            return dve.tensor_tensor(dst, src, rb.unsqueeze(1).to_broadcast([P, a, SEQ]), ALU.mult)

        def x_ready(pe, n):
            def after(kt):
                if kt == 2 and n:
                    flip(pe, n, 1, 1)
                if kt % 2 == 0:
                    pe.wait_ge(*when("x_lo", (n, kt // 2)))
            return after

        def residual(dve, n, c_last, scale=1.0):
            for nn in range(2):
                for t in range(TT):
                    if (t, nn) == (1, 1):
                        if n + 1 not in (BRIDGE, N_NORMS - 1):
                            x_low(dve, n + 1, 0)
                        used(dve, c_last)
                    else:
                        dve.wait_ge(*when("acc_done", (c_last, t, nn)))
                    hv = h[:, t, nn * 512:(nn + 1) * 512]
                    dve.scalar_tensor_tensor(hv, acc[:, 2 * t + nn, :], scale, hv,
                                             ALU.mult, ALU.add).then_inc(*sig("h_new", (n + 1, t, nn)))

        def repeat(eng, turns, last_phase, body):
            apart = 1 if last_phase else 0
            with eng.Fori(0, turns - apart) as i:
                body(i)
            for i in range(turns - apart, turns):
                body(i)

        def zero_acc(pe, c):
            for b in range(4):
                pe.matmul(acc[:, b, :], zero[:, 0:P], zero[:, :], start=True, stop=False)

        def down(pe, c, k_slot, i=0, last=False, before_last=None):
            rows(pe, c, acc_tn, lambda kt: hid[:, k_slot, kt, :, :], 2, 2, False, last, i, wide,
                 acc_done=c if last else None, before_last=before_last)

        def up(pe, c, bank, i=0, after=None):
            columns(pe, c, lambda f: tb[:, bank, f * SEQ:(f + 1) * SEQ], 2, KT, SEQ, i, after=after)

        def mlp_pe(pe, l, c, n):
            bu = BU[("mlp", l)]
            up(pe, c, 0, after=x_ready(pe, n))
            if l == 0:
                pe.wait_ge(*when("zeroed", 0))
            zero_acc(pe, c)
            spread(pe, n)
            with pe.Fori(0, (PAIRS_A - 1) // 3) as i:
                for j in range(3):
                    if j == 2:
                        pe.wait_ge(hid_u, bu + 1 + 3 * i)
                    up(pe, c + 1 + 2 * j, (j + 1) % 3, i)
                    pe.wait_ge(hid_lo, HT[("mlp", l)] + 1 + j + 3 * i)
                    down(pe, c + 2 + 2 * j, j, i)
            pe.wait_ge(hid_lo, HT[("mlp", l)] + PAIRS_A)
            down(pe, c + CHUNKS_MLP - 1, (PAIRS_A - 1) % 3, last=True, before_last=flip_lower(pe, n))

        def mlp_act(act, l, c, n):
            base = HT[("mlp", l)]

            def hidden(k, i=0):
                act.wait_ge(hid_t, base + 1 + k + 3 * i)
                s = k % 3
                act.activation(hid[:, s, :, 0, :], f_hid.rearrange("p (f t) -> p f t", f=2), ACT.Copy).then_inc(hid_hi, 1)

            hidden(0)
            split_hi(act, c, SPLIT)
            with act.Fori(0, (PAIRS_A - 1) // 3) as i:
                for j in range(3):
                    hidden(j + 1, i)
                    split_hi(act, c, 1 + 2 * j + SPLIT, i)
                    split_hi(act, c, 2 + 2 * j + SPLIT, i)

        def mlp_dve(dve, l, c, n):
            base = HT[("mlp", l)]

            def hidden(k, j, i=0):
                used(dve, c + j, i)
                if k:
                    dve.wait_ge(hid_lo, base + k + 3 * i)
                by_rb(dve, two(f_up), two(tb[:, k % 3, :]), n, k == 0).then_inc(hid_u, 1)
                dve.wait_ge(hid_u, BU[("mlp", l)] + 1 + k + 3 * i)
                dve.scalar_tensor_tensor(f_hid, f_up, 0.0, f_up, ALU.max, ALU.mult).then_inc(hid_t, 1)
                dve.wait_ge(hid_hi, base + 1 + k + 3 * i)
                dve.tensor_tensor(hid[:, k % 3, :, 1, :], f_hid.rearrange("p (f t) -> p f t", f=2),
                                  hid[:, k % 3, :, 0, :], ALU.subtract).then_inc(hid_lo, 1)

            hidden(0, 0)
            with dve.Fori(0, (PAIRS_A - 1) // 3) as i:
                for j in range(3):
                    split_lo(dve, c, 2 * j + SPLIT, i)
                    hidden(j + 1, 1 + 2 * j, i)
                    split_lo(dve, c, 1 + 2 * j + SPLIT, i)
            residual(dve, n, c + CHUNKS_MLP - 1)

        def ffn_pe(pe, f, c, n):
            base = HT[("ffn", f)]
            up(pe, c, 0, after=x_ready(pe, n))
            zero_acc(pe, c)
            up(pe, c + 1, 1)
            spread(pe, n)

            def turn(i):
                for j in range(2):
                    k = j + 1
                    if j == 1:
                        pe.wait_ge(hid_t, base + 1 + 2 * i)
                    up(pe, c + 2 + 3 * j, 2 * (k % 2), i)
                    if j == 0:
                        pe.wait_ge(*when("rb", n))
                    up(pe, c + 3 + 3 * j, 2 * (k % 2) + 1, i)
                    pe.wait_ge(hid_lo, base + 1 + j + 2 * i)
                    down(pe, c + 4 + 3 * j, j, i)

            repeat(pe, (PAIRS_B - 1) // 2, f == 2 * DEPTH_B - 1, turn)
            pe.wait_ge(hid_lo, base + PAIRS_B)
            down(pe, c + CHUNKS_FFN - 1, (PAIRS_B - 1) % 2, last=True, before_last=flip_lower(pe, n))

        def ffn_act(act, f, c, n):
            base, bu = HT[("ffn", f)], BU[("ffn", f)]

            def hidden(k, i=0):
                act.wait_ge(hid_u, bu + 1 + k + 2 * i)
                act.activation(f_act, f_gate, ACT.Silu).then_inc(hid_g, 1)
                act.wait_ge(hid_t, base + 1 + k + 2 * i)
                act.activation(hid[:, k % 2, :, 0, :], two(f_hid), ACT.Copy).then_inc(hid_hi, 1)

            split_hi(act, c, SPLIT)
            hidden(0)
            split_hi(act, c, 1 + SPLIT)

            def turn(i):
                for j in range(2):
                    split_hi(act, c, 2 + 3 * j + SPLIT, i)
                    hidden(j + 1, i)
                    split_hi(act, c, 3 + 3 * j + SPLIT, i)
                    split_hi(act, c, 4 + 3 * j + SPLIT, i)

            repeat(act, (PAIRS_B - 1) // 2, f == 2 * DEPTH_B - 1, turn)

        def ffn_dve(dve, f, c, n):
            base, bu, bg = HT[("ffn", f)], BU[("ffn", f)], BG[("ffn", f)]

            def gate(k, j, i=0):
                used(dve, c + j, i)
                if k:
                    dve.wait_ge(hid_g, bg + k + 2 * i)
                by_rb(dve, two(f_gate), two(tb[:, 2 * (k % 2), :]), n, k == 0).then_inc(hid_u, 1)

            def hidden(k, j, i=0):
                used(dve, c + j, i)
                by_rb(dve, two(f_up), two(tb[:, 2 * (k % 2) + 1, :]), n, False).then_inc(hid_v, 1)
                dve.wait_ge(hid_v, bg + 1 + k + 2 * i)
                dve.wait_ge(hid_g, bg + 1 + k + 2 * i)
                if k:
                    dve.wait_ge(hid_lo, base + k + 2 * i)
                dve.tensor_tensor(f_hid, f_up, f_act, ALU.mult).then_inc(hid_t, 1)
                dve.wait_ge(hid_hi, base + 1 + k + 2 * i)
                dve.tensor_tensor(hid[:, k % 2, :, 1, :], two(f_hid), hid[:, k % 2, :, 0, :],
                                  ALU.subtract).then_inc(hid_lo, 1)

            gate(0, 0)
            split_lo(dve, c, SPLIT)
            hidden(0, 1)

            def turn(i):
                for j in range(2):
                    split_lo(dve, c, 1 + 3 * j + SPLIT, i)
                    gate(j + 1, 2 + 3 * j, i)
                    split_lo(dve, c, 2 + 3 * j + SPLIT, i)
                    hidden(j + 1, 3 + 3 * j, i)
                    split_lo(dve, c, 3 + 3 * j + SPLIT, i)

            repeat(dve, (PAIRS_B - 1) // 2, f == 2 * DEPTH_B - 1, turn)
            residual(dve, n, c + CHUNKS_FFN - 1, 0.5)

        HT, BU, BG = {}, {}, {}
        at = [0, 0, 0]
        for kind, l, c, n in PHASES:
            if kind in ("mlp", "ffn"):
                HT[kind, l], BU[kind, l], BG[kind, l] = at
                at[0] += PAIRS_A if kind == "mlp" else PAIRS_B
                at[1] += PAIRS_A if kind == "mlp" else PAIRS_B
                at[2] += 0 if kind == "mlp" else PAIRS_B

        def ple_pe(pe, l, c, n):
            for j in range(4):
                pe.wait_ge(*when("x_lo", (n, j)))
                rows(pe, c + j, acc_tn, lambda kt: xT[:, 2 * j + kt, :, :], 2, 2, j == 0, j == 3,
                     view=wide, acc_done=("gate", c) if j == 3 else None,
                     before_last=(lambda: flip(pe, n, 1, 1)) if j == 0 else None)
            pe.wait_ge(*when("p_lo", l))
            rows(pe, c + 4, lambda t, nn: tb[:, 2 * nn + t, :], lambda kt: cat[:, 6 + kt, :, :], 2, 2, True, True, view=wide,
                 acc_done=c + 4, before_last=flip_lower(pe, n))

        def ple_act(act, l, c, n):
            act.wait_ge(*when("p_in", l))
            act.activation(cat[:, 6:8, 0, :], p_in, ACT.Copy).then_inc(*sig("p_hi", l))
            for j in range(4):
                split_hi(act, c, j + SPLIT)
            act.wait_ge(*when("rstd", n))
            for nn in range(2):
                for t in range(TT):
                    if (t, nn) == (1, 1):
                        used(act, c + 3)
                    else:
                        act.wait_ge(*when("acc_done", (("gate", c), t, nn)))
                    act.activation(xn[:, t, nn * 512:(nn + 1) * 512], acc[:, 2 * t + nn, :], ACT.Sigmoid,
                                   scale=rstd[:, t:t + 1]).then_inc(*sig("gate", (l, t, nn)))

        def ple_dve(dve, l, c, n):
            dve.wait_ge(*when("p_hi", l))
            dve.tensor_tensor(cat[:, 6:8, 1, :], p_in, cat[:, 6:8, 0, :], ALU.subtract).then_inc(*sig("p_lo", l))
            for j in range(3):
                split_lo(dve, c, j + SPLIT)
            for nn in range(2):
                for t in range(TT):
                    if (t, nn) == (1, 1):
                        if n + 1 != BRIDGE:
                            x_low(dve, n + 1, 0)
                        used(dve, c + 4)
                    else:
                        dve.wait_ge(*when("acc_done", (c + 4, t, nn)))
                    dve.wait_ge(*when("gate", (l, t, nn)))
                    g, hv = xn[:, t, nn * 512:(nn + 1) * 512], h[:, t, nn * 512:(nn + 1) * 512]
                    dve.tensor_tensor(g, tb[:, 2 * nn + t, :], g, ALU.mult).then_inc(*sig("own", ("ple", l, t, nn)))
                    dve.wait_ge(*when("own", ("ple", l, t, nn)))
                    dve.tensor_tensor(hv, hv, g, ALU.add).then_inc(*sig("h_new", (n + 1, t, nn)))

        def score_map(pe, bank, q, k, key):
            b = tb[:, bank, :]
            pe.matmul(b[:, 0:P], q[:, 0:P], k[:, 0:P], start=True, stop=False)
            pe.matmul(b[:, 0:P], ident_b, causal_b, start=False, stop=True)
            pe.matmul(b[:, P:P + SEQ], q[:, P:SEQ], k, start=True, stop=True)
            pe.matmul(b[:, 2 * P:3 * P], ident_b, causal_b, start=False, stop=True, skip_group_check=True).then_inc(*sig("scores", key))

        def map_stats(dve, m, bank, key, scale):
            dve.wait_ge(*when("scores", key))
            dve.tensor_reduce(mx[:, m, 0:1], tb[:, bank, 0:P], AX.X, ALU.max)
            dve.tensor_reduce(mx[:, m, 1:2], tb[:, bank, P:CAUSAL], AX.X, ALU.max).then_inc(*sig("own", ("mx", key)))
            dve.wait_ge(*when("own", ("mx", key)))
            dve.tensor_scalar(nmx[:, m, :], mx[:, m, :], -scale, None, ALU.mult).then_inc(*sig("top", key))

        def map_exp(act, m, bank, dst, key, scale):
            act.wait_ge(*when("top", key))
            act.activation(dst[:, 0:P], tb[:, bank, 0:P], ACT.Exp, bias=nmx[:, m, 0:1], scale=scale,
                           accum_out=sm[:, m, 0:1])
            act.activation(dst[:, P:CAUSAL], tb[:, bank, P:CAUSAL], ACT.Exp, bias=nmx[:, m, 1:2], scale=scale,
                           accum_out=sm[:, m, 1:2]).then_inc(*sig("exps", key))

        def map_transpose(pe, bank, src, key):
            for j in range(3):
                last = pe.transpose(tb[:, bank, j * P:(j + 1) * P], src[:, j * P:(j + 1) * P], ident)
            last.then_inc(*sig("flipped", key))

        def heads_out(pe, i, hd, v, w):
            g, p0, at = hd // 4, HD * (hd % 2), SEQ * (hd % 4 // 2)
            if hd % 4 == 0 and g >= 2:
                pe.wait_ge(*when("cat_lo", (i, g - 2)))
            o = acc[p0:p0 + HD, g % 2, at:at + SEQ]
            pe.matmul(o, v[:, 0, hd * HD:(hd + 1) * HD], w[:, 0:SEQ], start=True, stop=True)
            pe.matmul(o[:, P:SEQ], v[:, 1, hd * HD:(hd + 1) * HD], w[:, SEQ:CAUSAL], start=False,
                      stop=True, skip_group_check=True).then_inc(*sig("head_out", (i, hd)))

        def cat_hi(act, i, g):
            act.wait_ge(*when("head_out", (i, 4 * g + 3)))
            act.activation(cat[:, 2 * g:2 * g + 2, 0, :], two(acc[:, g % 2, :]), ACT.Copy).then_inc(*sig("cat_hi", (i, g)))

        def cat_lo(dve, i, g):
            dve.wait_ge(*when("cat_hi", (i, g)))
            dve.tensor_tensor(cat[:, 2 * g:2 * g + 2, 1, :], two(acc[:, g % 2, :]), cat[:, 2 * g:2 * g + 2, 0, :],
                              ALU.subtract).then_inc(*sig("cat_lo", (i, g)))

        def project_out(pe, i, c, n):
            for g in range(4):
                pe.wait_ge(*when("cat_lo", (i, g)))
            for j in range(4):
                rows(pe, c + j, acc_tn, lambda kt: cat[:, 2 * j + kt, :, :], 2, 2, j == 0, j == 3, view=wide,
                     acc_done=c + 3 if j == 3 else None, before_last=flip_lower(pe, n) if j == 3 else None)

        UNITS = KT * 2

        def plan(turned, per_step, ahead):
            seq = []
            for e in range(2, 8):
                for u in range(UNITS):
                    if turned and u == 4:
                        seq.append(("rotate", e - 1))
                    seq.append(("product", e, u))
            if turned:
                seq.append(("rotate", 7))
            first, rest = seq[:ahead], seq[ahead:]
            return first, [rest[k:k + per_step] for k in range(0, len(rest), per_step)]

        PLAN = {"moba": plan(True, 9, 5), "stick": plan(False, 18, 0)}

        class Feed:

            def __init__(self, pe, kind, i, c):
                self.pe, self.kind, self.i, self.c = pe, kind, i, c
                self.first, self.steps = PLAN[kind]
                self.left, self.at = [], None

            def product(self, e, u):
                pe, i = self.pe, self.i
                if u == 0:
                    if e >= 2:
                        pe.wait_ge(*when("turned" if self.kind == "moba" else "taken", (i, e - 2)))
                    self.at = columns_by_steps(pe, self.c + 4 + e, lambda f: acc[:, 2 + e % 2, f * SEQ:(f + 1) * SEQ],
                                               2, KT, SEQ)
                next(self.at, None)
                if u == UNITS - 1:
                    next(self.at, None)

            def rotate(self, e):
                self.pe.wait_ge(*when("taken", (self.i, e)))
                self.pe.matmul(acc[:, 2 + e % 2, :], rot, q_or_k(e), start=True, stop=True)\
                    .then_inc(*sig("rotated", (self.i, e)))

            def run(self, units):
                for unit in units:
                    (self.product if unit[0] == "product" else self.rotate)(*unit[1:])

            def begin(self):
                for e in range(2):
                    for u in range(UNITS):
                        if self.kind == "moba" and e == 1 and u == 4:
                            self.rotate(0)
                        self.product(e, u)
                self.run(self.first)

            def step(self, s):
                self.left = list(self.steps[s]) if s < len(self.steps) else []

            def some(self, part):
                n = -(-len(self.left) // part)
                self.run(self.left[:n])
                self.left = self.left[n:]

        class NoFeed:
            def step(self, s):
                pass

            def some(self, part):
                pass

        def take_dve(dve, kind, i, c, n, e):
            used(dve, c + 4 + e)
            by_rb(dve, two(q_or_k(e)), two(acc[:, 2 + e % 2, :]), n, e == 0).then_inc(*sig("taken", (i, e)))
            split_lo(dve, c, 4 + e + SPLIT)

        def turn_dve(dve, i, e):
            b, r = two(q_or_k(e)), two(rot_a)
            cos = cst[:, C_COSM:C_COSM + SEQ].unsqueeze(1).to_broadcast([P, 2, SEQ])
            sin = cst[:, C_SINM:C_SINM + SEQ].unsqueeze(1).to_broadcast([P, 2, SEQ])
            dve.wait_ge(*when("rotated", (i, e)))
            if e:
                dve.wait_ge(*when("turned", (i, e - 1)))
            dve.tensor_tensor(r, two(acc[:, 2 + e % 2, :]), sin, ALU.mult)
            dve.tensor_tensor(b, b, cos, ALU.mult).then_inc(*sig("own", ("turn", i, e)))
            dve.wait_ge(*when("own", ("turn", i, e)))
            dve.tensor_tensor(b, b, r, ALU.add).then_inc(*sig("turned", (i, e)))

        def feed_act(act, kind, i, c, units):
            for unit in units:
                if unit[0] == "product" and unit[2] == UNITS - 1:
                    split_hi(act, c, 4 + unit[1] + SPLIT)

        def feed_dve(dve, kind, i, c, n, units):
            for unit in units:
                if unit[0] == "product" and unit[2] == UNITS - 1:
                    take_dve(dve, kind, i, c, n, unit[1])
                if unit[0] == "rotate":
                    turn_dve(dve, i, unit[1])

        def q_or_k(e):
            b = b_k if e % 2 else b_q
            return b[:, 2 * (e // 2):2 * (e // 2) + 2, :].rearrange("p a t -> p (a t)")

        def v_bank(t, n_):
            return acc[:, t, :] if n_ == 0 else tb[:, t, :]

        def qkv_pe(pe, kind, i, c, n):
            for j in range(4):
                rows(pe, c + j, lambda t, nn: v_bank(t, j // 2)[:, (j % 2) * SEQ:(j % 2 + 1) * SEQ],
                     lambda kt: xT[:, kt, :, :], KT, 1, True, True, view=half,
                     after=x_ready(pe, n) if j == 0 else None)
                if j == 1:
                    spread(pe, n)
            feed = Feed(pe, kind, i, c)
            feed.begin()
            pe.wait_ge(*when("rb", n))
            pe.wait_ge(*when("v_out", (i, 1)))
            return feed

        def qkv_act(act, kind, i, c, n):
            for j in range(4):
                if j % 2 == 1:
                    used(act, c + j)
                    for t in range(TT):
                        last = act.activation(b_v[:, t, (j // 2) * 512:(j // 2 + 1) * 512], v_bank(t, j // 2), ACT.Copy,
                                              scale=rstd[:, t:t + 1])
                    last.then_inc(*sig("v_out", (i, j // 2)))
                split_hi(act, c, j + SPLIT)
            for e in range(2):
                split_hi(act, c, 4 + e + SPLIT)
            feed_act(act, kind, i, c, PLAN[kind][0])

        def qkv_dve(dve, kind, i, c, n):
            for j in range(4):
                split_lo(dve, c, j + SPLIT)
            for e in range(2):
                take_dve(dve, kind, i, c, n, e)
                if kind == "moba" and e == 1:
                    turn_dve(dve, i, 0)
            feed_dve(dve, kind, i, c, n, PLAN[kind][0])

        def of_head(buf):
            return lambda hd: buf[HD * (hd % 2):HD * (hd % 2 + 1), hd // 2, :]

        def softmax_pe(pe, i, c_out, n, q, k, v, p_T, feed, group_ready):
            for s in range(HEADS + 3):
                feed.step(s)
                if s < HEADS:
                    if s % 4 == 0:
                        group_ready(s // 4)
                    if s >= 2:
                        pe.wait_ge(*when("exps", (i, s - 2)))
                    score_map(pe, s % 2, q(s), k(s), (i, s))
                feed.some(3)
                if 2 <= s < HEADS + 2:
                    m = s - 2
                    pe.wait_ge(*when("weights", (i, m)))
                    if m >= 2:
                        pe.wait_ge(*when("flip_out", (i, m - 2)))
                    map_transpose(pe, 2 + m % 2, probs[:, m % 4, :], (i, m))
                feed.some(2)
                if s >= 3:
                    m = s - 3
                    pe.wait_ge(*when("flip_out", (i, m)))
                    heads_out(pe, i, m, v, p_T[m % 2])
                feed.some(1)
            project_out(pe, i, c_out, n)

        def softmax_act(act, i, scale, p_T, behind):
            for s in range(HEADS + 4):
                if s < HEADS:
                    if s >= 4:
                        act.wait_ge(*when("flipped", (i, s - 4)))
                    map_exp(act, s, s % 2, probs[:, s % 4, :], (i, s), scale)
                if 2 <= s < HEADS + 2:
                    m = s - 2
                    act.wait_ge(*when("flipped", (i, m)))
                    if m >= 2:
                        act.wait_ge(*when("head_out", (i, m - 2)))
                    act.activation(p_T[m % 2], tb[:, 2 + m % 2, 0:CAUSAL], ACT.Copy).then_inc(*sig("flip_out", (i, m)))
                if s >= 7 and (s - 7) % 4 == 0:
                    cat_hi(act, i, (s - 7) // 4)
                behind(s)

        def softmax_dve(dve, i, scale, behind):
            for s in range(HEADS + 4):
                if s < HEADS:
                    map_stats(dve, s, s % 2, (i, s), scale)
                if 1 <= s <= HEADS:
                    m = s - 1
                    dve.wait_ge(*when("exps", (i, m)))
                    dve.reciprocal(rs[:, m, :], sm[:, m, :]).then_inc(*sig("own", ("rs", i, m)))
                    dve.wait_ge(*when("own", ("rs", i, m)))
                    pr = probs[:, m % 4, :]
                    dve.tensor_scalar(pr[:, 0:P], pr[:, 0:P], rs[:, m, 0:1], None, ALU.mult)
                    dve.tensor_scalar(pr[:, P:CAUSAL], pr[:, P:CAUSAL], rs[:, m, 1:2], None,
                                      ALU.mult).then_inc(*sig("weights", (i, m)))
                if s >= 7 and (s - 7) % 4 == 0:
                    cat_lo(dve, i, (s - 7) // 4)
                behind(s)

        def moba_pe(pe, i, c, n):
            feed = qkv_pe(pe, "moba", i, c, n)
            softmax_pe(pe, i, c + 12, n, of_head(b_q), of_head(b_k), b_v, m_pT, feed,
                       lambda g: pe.wait_ge(*when("turned", (i, 2 * g + 1))))

        def moba_act(act, i, c, n):
            qkv_act(act, "moba", i, c, n)
            steps = PLAN["moba"][1]
            softmax_act(act, i, HD ** -0.5, m_pT, lambda s: feed_act(act, "moba", i, c, steps[s] if s < len(steps) else []))
            for j in range(12, 15):
                split_hi(act, c, j + SPLIT)

        def moba_dve(dve, i, c, n):
            qkv_dve(dve, "moba", i, c, n)
            steps = PLAN["moba"][1]
            softmax_dve(dve, i, HD ** -0.5, lambda s: feed_dve(dve, "moba", i, c, n, steps[s] if s < len(steps) else []))
            for j in range(12, 14):
                split_lo(dve, c, j + SPLIT)
            residual(dve, n, c + 15)

        def z_banks(p):
            return tb[:, 2 * (p % 2):2 * (p % 2) + 2, 0:CAUSAL]

        def stick_pe(pe, i, c, n):
            feed = qkv_pe(pe, "stick", i, c, n)
            q, k = of_head(b_q), of_head(b_k)
            for p in range(HEADS // 2 + 2):
                feed.step(p)
                if p < HEADS // 2:
                    if p % 2 == 0:
                        pe.wait_ge(*when("taken", (i, p + 1)))
                    if p >= 2:
                        pe.wait_ge(*when("sticks", (i, p - 2)))
                    for u in range(2):
                        z, hd = tb[:, 2 * (p % 2) + u, :], 2 * p + u
                        pe.matmul(z[:, 0:SEQ], k(hd)[:, 0:P], q(hd), start=True, stop=True)
                        last = pe.matmul(z[:, SEQ:CAUSAL], k(hd)[:, P:SEQ], q(hd)[:, P:SEQ], start=False, stop=True,
                                         skip_group_check=True)
                    last.then_inc(*sig("scores", (i, p)))
                feed.some(3)
                if 1 <= p <= HEADS // 2:
                    m = p - 1
                    pe.wait_ge(*when("keeps", (i, m)))
                    for u in range(2):
                        z, L = tb[:, 2 * (m % 2) + u, :], s_l[m % 2][:, u, :]
                        pe.matmul(z[:, 0:SEQ], tri, L[:, 0:SEQ], start=False, stop=True, skip_group_check=True)
                        pe.matmul(z[:, P:SEQ], every, L[:, SEQ:CAUSAL], start=False, stop=True, skip_group_check=True)
                        pe.matmul(z[:, SEQ:CAUSAL], tri, L[:, SEQ:CAUSAL], start=False, stop=True, skip_group_check=True)
                        pe.matmul(z[:, 0:P], ident_b, strict_b, start=False, stop=True, skip_group_check=True)
                        last = pe.matmul(z[:, SEQ:CAUSAL], ident_b, strict_b, start=False, stop=True, skip_group_check=True)
                    last.then_inc(*sig("tails", (i, m)))
                feed.some(2)
                if p >= 2:
                    m = p - 2
                    pe.wait_ge(*when("sticks", (i, m)))
                    for u in range(2):
                        heads_out(pe, i, 2 * m + u, b_v, s_w[m % 2][:, u, :])
                feed.some(1)
            project_out(pe, i, c + 12, n)

        def stick_act(act, i, c, n):
            qkv_act(act, "stick", i, c, n)
            scale = HD ** -0.5
            steps = PLAN["stick"][1]
            for p in range(HEADS // 2 + 2):
                if p < HEADS // 2:
                    e = s_e[p % 2]
                    act.wait_ge(*when("z_neg", (i, p)))
                    act.activation(e, e, ACT.Exp, scale=scale).then_inc(*sig("own_act", ("e", i, p)))
                if 1 <= p <= HEADS // 2:
                    m = p - 1
                    act.wait_ge(*when("tails", (i, m)))
                    if m >= 2:
                        act.wait_ge(*when("head_out", (i, 2 * (m - 2) + 1)))
                    act.activation(s_w[m % 2], z_banks(m), ACT.Exp, scale=scale).then_inc(*sig("sticks", (i, m)))
                if p < HEADS // 2:
                    act.wait_ge(*when("own_act", ("e", i, p)))
                    act.activation(e, e, ACT.Ln, bias=1.0).then_inc(*sig("soft", (i, p)))
                if p >= 3 and p % 2 == 1:
                    cat_hi(act, i, (p - 3) // 2)
                feed_act(act, "stick", i, c, steps[p] if p < len(steps) else [])
            for j in range(12, 15):
                split_hi(act, c, j + SPLIT)

        def stick_dve(dve, i, c, n):
            qkv_dve(dve, "stick", i, c, n)
            scale = HD ** -0.5
            steps = PLAN["stick"][1]
            for p in range(HEADS // 2 + 2):
                if p < HEADS // 2:
                    e, L = s_e[p % 2], s_l[p % 2]
                    dve.wait_ge(*when("scores", (i, p)))
                    if p >= 2:
                        dve.wait_ge(*when("tails", (i, p - 2)))
                    dve.tensor_scalar(L, z_banks(p), 0.0, None, ALU.max).then_inc(*sig("own", ("l", i, p)))
                    dve.wait_ge(*when("own", ("l", i, p)))
                    dve.scalar_tensor_tensor(e, L, -2.0, z_banks(p), ALU.mult, ALU.add).then_inc(*sig("z_neg", (i, p)))
                    dve.wait_ge(*when("soft", (i, p)))
                    dve.scalar_tensor_tensor(L, L, scale, e, ALU.mult, ALU.add).then_inc(*sig("own", ("m", i, p)))
                    dve.wait_ge(*when("own", ("m", i, p)))
                    own_keys = strict.unsqueeze(1).to_broadcast([P, 2, P])
                    dve.tensor_tensor(L[:, :, 0:P], L[:, :, 0:P], own_keys, ALU.mult)
                    dve.tensor_tensor(L[:, :, SEQ:CAUSAL], L[:, :, SEQ:CAUSAL], own_keys, ALU.mult).then_inc(*sig("keeps", (i, p)))
                if p >= 3 and p % 2 == 1:
                    cat_lo(dve, i, (p - 3) // 2)
                feed_dve(dve, "stick", i, c, n, steps[p] if p < len(steps) else [])
            for j in range(12, 14):
                split_lo(dve, c, j + SPLIT)
            residual(dve, n, c + 15)

        lat = xn[:, :, 0:MLA_IN]
        LAT = [(0, MLA_QR), (MLA_QR, MLA_QR + MLA_KVR)]
        LAT_T = [(0, P), (P, P), (2 * P, P), (3 * P, P), (4 * P, P), (MLA_IN - MLA_HD, MLA_HD)]
        PAIRS = HEADS // 2
        q_of_pair = [(g, hd) for g, m in enumerate(MLA_Q_GROUPS) for hd in range(0, m, 2)]
        last_pair = {g: max(p for p, (gg, _) in enumerate(q_of_pair) if gg == g) for g in range(3)}
        kr_buf = cut(8192, SEQ)
        kr_rot = cut(8192 + SEQ, SEQ)

        def mla_pe(pe, i, c, n):
            for j in range(3):
                rows(pe, c + j, lambda t, nn: acc[:, (t if j < 2 else 2 + t), (j % 2) * SEQ:(j % 2 + 1) * SEQ],
                     lambda kt: xT[:, kt, :, :], KT, 1, True, True, view=half,
                     after=x_ready(pe, n) if j == 0 else None)
                if j == 1:
                    spread(pe, n)
            for j, (at_, m) in enumerate(LAT_T):
                if j in (0, 3):
                    pe.wait_ge(*when("lat_normed", (i, j // 3)))
                for t in range(TT):
                    last = pe.transpose(tb[0:m, j // 2, (j % 2) * SEQ + t * P:(j % 2) * SEQ + (t + 1) * P],
                                        lat[:, t, at_:at_ + m], ident)
                if j % 2 == 1:
                    last.then_inc(*sig("lat_T", (i, j // 2)))
            pe.wait_ge(*when("rb", n))
            pe.wait_ge(*when("kr_in", i))
            pe.matmul(tb[0:MLA_HD, 3, 0:SEQ], rotl[0:MLA_HD, 0:MLA_HD], kr_buf[0:MLA_HD, :], start=True,
                      stop=True).then_inc(*sig("kr_rot", i))
            pe.wait_ge(*when("lat_lo", (i, 2)))
            pe.wait_ge(*when("kr_done", i))
            for p in range(PAIRS + 1):
                if p < PAIRS:
                    g, h0 = q_of_pair[p]
                    if p >= 2:
                        pe.wait_ge(*when("pair_taken", (i, p - 2)))
                    pe.wait_ge(lo_done, c + 3 + g + 1)
                    s = (c + 3 + g) % SPLIT
                    width = MLA_Q_GROUPS[g] * MLA_HD
                    for u in range(2):
                        o = tb[0:MLA_HD, p % 2, u * SEQ:(u + 1) * SEQ]
                        for kt in range(3):
                            a = kt * width + (h0 + u) * MLA_HD
                            hi, lo = w_hi[:, s, a:a + MLA_HD], w_lo[:, s, a:a + MLA_HD]
                            pe.matmul(o, hi, xT[:, kt, 0, :], start=kt == 0, stop=False)
                            pe.matmul(o, hi, xT[:, kt, 1, :], start=False, stop=False)
                            last = pe.matmul(o, lo, xT[:, kt, 0, :], start=False, stop=kt == 2)
                    if p == last_pair[g]:
                        last.then_inc(chunk_used, 1)
                    else:
                        last.then_inc(*sig("pair_done", (i, p)))
                if p >= 1:
                    m = p - 1
                    pe.wait_ge(*when("pair_taken", (i, m)))
                    if m >= 2:
                        pe.wait_ge(*when("turned", (i, m - 2)))
                    pe.matmul(acc[0:MLA_HD, m % 2, :], rotl[0:MLA_HD, 0:MLA_HD],
                              m_q[0:MLA_HD, 2 * m:2 * m + 2, :].rearrange("p a t -> p (a t)"),
                              start=True, stop=True).then_inc(*sig("rotated", (i, m)))
            for g in range(2):
                pe.wait_ge(lo_done, c + 6 + g + 1)
                s = (c + 6 + g) % SPLIT
                for p in range(4):
                    pp = PAIRS + 4 * g + p
                    pe.wait_ge(*when("pair_taken", (i, pp - 2)))
                    for u in range(2):
                        o = tb[:, pp % 2, u * SEQ:(u + 1) * SEQ]
                        for kt in range(2):
                            a = kt * D + (2 * p + u) * P
                            hi, lo = w_hi[:, s, a:a + P], w_lo[:, s, a:a + P]
                            pe.matmul(o, hi, xT[:, 3 + kt, 0, :], start=kt == 0, stop=False)
                            pe.matmul(o, hi, xT[:, 3 + kt, 1, :], start=False, stop=False)
                            last = pe.matmul(o, lo, xT[:, 3 + kt, 0, :], start=False, stop=kt == 1)
                    last.then_inc(*sig("pair_done", (i, pp)))
                if g == 0:
                    pe.wait_ge(*when("turned", (i, PAIRS - 1)))

                def v_cols(w, s_, kt, nn):
                    return w[:, s_, kt * D:(kt + 1) * D].rearrange("p (h e) -> p h e", e=P)[:, :, HD:P]

                rows(pe, c + 6 + g, lambda t, nn: acc[:, 2 * t + g, :], lambda kt: xT[:, 3 + kt, :, :], 2, 1,
                     True, True, view=v_cols)
            pe.wait_ge(*when("pair_taken", (i, 2 * PAIRS - 1)))
            pe.wait_ge(*when("v_out", (i, 1)))
            softmax_pe(pe, i, c + 8, n, lambda hd: m_q[0:MLA_HD, hd, :], lambda hd: m_k[0:MLA_HD, hd, :], m_v, l_pT,
                       NoFeed(), lambda g: None)

        def mla_act(act, i, c, n):
            for k_ in range(2):
                split_hi(act, c, k_ + SPLIT)
                act.wait_ge(*when("lat_in", (i, k_)))
                a, b = LAT[k_]
                for t in range(TT):
                    last = act.activation(cut(512 * t, b - a), lat[:, t, a:b], ACT.Square,
                                          accum_out=s8[2][:, 2 * k_ + t:2 * k_ + t + 1])
                last.then_inc(*sig("lat_ss", (i, k_)))
                act.wait_ge(*when("lat_ms", (i, k_)))
                act.activation(s8[1][:, 2 * k_:2 * k_ + 2], s8[0][:, 2 * k_:2 * k_ + 2], ACT.Sqrt)\
                    .then_inc(*sig("root", ("mla", i, k_)))
            split_hi(act, c, 2 + SPLIT)
            for b in range(3):
                act.wait_ge(*when("lat_T", (i, b)))
                if b < 2:
                    act.activation(xT[:, 2 * b:2 * b + 2, 0, :], tb[:, b, :].rearrange("p (k t) -> p k t", k=2),
                                   ACT.Copy).then_inc(*sig("lat_hi", (i, b)))
                else:
                    act.activation(kr_buf[0:MLA_HD, :], tb[0:MLA_HD, 2, SEQ:2 * SEQ], ACT.Copy).then_inc(*sig("kr_in", i))
                    act.activation(xT[:, 4, 0, :], tb[:, 2, 0:SEQ], ACT.Copy).then_inc(*sig("lat_hi", (i, 2)))
            for p in range(2 * PAIRS):
                if p < PAIRS and p == last_pair[q_of_pair[p][0]]:
                    used(act, c + 3 + q_of_pair[p][0])
                else:
                    act.wait_ge(*when("pair_done", (i, p)))
                b = m_q if p < PAIRS else m_k
                m = MLA_HD if p < PAIRS else HD
                hd = 2 * (p % PAIRS)
                act.activation(b[0:m, hd:hd + 2, :], tb[0:m, p % 2, :].rearrange("p (a t) -> p a t", a=2),
                               ACT.Copy).then_inc(*sig("pair_taken", (i, p)))
                if p < PAIRS and p == last_pair[q_of_pair[p][0]]:
                    split_hi(act, c, 3 + q_of_pair[p][0] + SPLIT)
                if p in (PAIRS + 3, 2 * PAIRS - 1):
                    g = (p - PAIRS) // 4
                    used(act, c + 6 + g)
                    if g == 0:
                        act.wait_ge(*when("k_rope", i))
                    for t in range(TT):
                        last = act.activation(m_v[:, t, g * 512:(g + 1) * 512], acc[:, 2 * t + g, :], ACT.Copy)
                    last.then_inc(*sig("v_out", (i, g)))
                    split_hi(act, c, 6 + g + SPLIT)
            softmax_act(act, i, MLA_HD ** -0.5, l_pT, lambda s: None)
            for j in range(8, 11):
                split_hi(act, c, j + SPLIT)

        def mla_dve(dve, i, c, n):
            split_lo(dve, c, SPLIT)
            for k_ in range(2):
                used(dve, c + 1 + k_)
                for t in range(TT):
                    if k_ == 0:
                        last = dve.tensor_scalar(lat[:, t, 0:512], acc[:, t, :], rstd[:, t:t + 1], None, ALU.mult)
                    else:
                        last = dve.tensor_scalar(lat[:, t, 512:MLA_IN], acc[:, 2 + t, SEQ - (MLA_IN - 512):SEQ],
                                                 rstd[:, t:t + 1], None, ALU.mult)
                last.then_inc(*sig("lat_in", (i, k_)))
                a, b = LAT[k_]
                two_ = slice(2 * k_, 2 * k_ + 2)
                if k_ == 0:
                    dve.wait_ge(*when("gain_in", "mla"))
                dve.wait_ge(*when("lat_ss", (i, k_)))
                dve.tensor_scalar(s8[0][:, two_], s8[2][:, two_], 1.0 / (b - a), EPS, ALU.mult, ALU.add).then_inc(*sig("lat_ms", (i, k_)))
                newton(dve, s8[1][:, two_], s8[0][:, two_], s8[3][:, two_], s8[4][:, two_], s8[5][:, two_], ("mla", i, k_))
                for t in range(TT):
                    last = dve.scalar_tensor_tensor(lat[:, t, a:b], lat[:, t, a:b], s8[5][:, 2 * k_ + t:2 * k_ + t + 1],
                                                    gain[:, a:b], ALU.mult, ALU.mult)
                last.then_inc(*sig("lat_normed", (i, k_)))
                split_lo(dve, c, 1 + k_ + SPLIT)
            for b in range(3):
                w = 2 if b < 2 else 1
                dve.wait_ge(*when("lat_hi", (i, b)))
                dve.tensor_tensor(xT[:, 2 * b:2 * b + w, 1, :], tb[:, b, 0:w * SEQ].rearrange("p (k t) -> p k t", k=w),
                                  xT[:, 2 * b:2 * b + w, 0, :], ALU.subtract).then_inc(*sig("lat_lo", (i, b)))
            R = slice(0, MLA_HD)
            cos, sin = cst[R, C_COSL:C_COSL + SEQ], cst[R, C_SINL:C_SINL + SEQ]
            dve.wait_ge(*when("kr_rot", i))
            dve.tensor_tensor(kr_rot[R, :], tb[R, 3, 0:SEQ], sin, ALU.mult)
            dve.tensor_tensor(kr_buf[R, :], kr_buf[R, :], cos, ALU.mult).then_inc(*sig("own", ("kr0", i)))
            dve.wait_ge(*when("own", ("kr0", i)))
            dve.tensor_tensor(kr_buf[R, :], kr_buf[R, :], kr_rot[R, :], ALU.add).then_inc(*sig("kr_done", i))
            dve.wait_ge(*when("kr_done", i))
            dve.tensor_copy(m_k[HD:MLA_HD, :, :], kr_buf[HD:MLA_HD, :].unsqueeze(1).to_broadcast([MLA_ROPE, HEADS, SEQ]))\
               .then_inc(*sig("k_rope", i))
            turn = xn[:, 1, 0:512].rearrange("p (a t) -> p a t", a=2)
            cos2, sin2 = cos.unsqueeze(1).to_broadcast([MLA_HD, 2, SEQ]), sin.unsqueeze(1).to_broadcast([MLA_HD, 2, SEQ])
            for p in range(PAIRS):
                g = q_of_pair[p][0]
                b = m_q[R, 2 * p:2 * p + 2, :]
                dve.wait_ge(*when("rotated", (i, p)))
                if p:
                    dve.wait_ge(*when("turned", (i, p - 1)))
                dve.tensor_tensor(turn[R, :, :], acc[R, p % 2, :].rearrange("p (a t) -> p a t", a=2), sin2, ALU.mult)
                dve.tensor_tensor(b, b, cos2, ALU.mult).then_inc(*sig("own", ("turn", i, p)))
                dve.wait_ge(*when("own", ("turn", i, p)))
                dve.tensor_tensor(b, b, turn[R, :, :], ALU.add).then_inc(*sig("turned", (i, p)))
                if p == last_pair[g]:
                    split_lo(dve, c, 3 + g + SPLIT)
            for g in range(2):
                split_lo(dve, c, 6 + g + SPLIT)
            softmax_dve(dve, i, MLA_HD ** -0.5, lambda s: None)
            for j in range(8, 10):
                split_lo(dve, c, j + SPLIT)
            residual(dve, n, c + 11)

        A_DST = [a_x, a_x, a_q, a_q, a_k, a_k, None, None, a_gr, a_gr]
        A_UNITS = 6

        def a_dst(j):
            d = A_DST[j]
            return d[:, 2 * (j % 2):2 * (j % 2) + 2, 3:3 + SEQ] if j < 2 else d[:, 2 * (j % 2):2 * (j % 2) + 2, :]

        def a_bank(j):
            return tb[:, j % 4, :] if j < 8 else acc[:, j % 2, :]

        def a_qk(j):
            return a_dst(j), tb[:, j % 4, :]

        def mix_a_pe(pe, l, c, n):
            def turn(j):
                pe.wait_ge(*when("a_taken", (l, j)))
                b, bank = a_qk(j)
                pe.matmul(bank, rot, b.rearrange("p a t -> p (a t)"), start=True, stop=True).then_inc(*sig("rotated", ("a", l, j)))

            for j in range(6):
                if j == 3:
                    pe.wait_ge(*when("rb", n))
                if j >= 4:
                    pe.wait_ge(*when("a_taken", (l, j - 4)))
                columns(pe, c + j, lambda f: tb[:, j % 4, f * SEQ:(f + 1) * SEQ], 2, KT, SEQ,
                        after=x_ready(pe, n) if j == 0 else None)
                if j == 1:
                    spread(pe, n)
            pe.wait_ge(*when("conv", (l, 3)))
            pe.wait_ge(*when("gates_in", l))
            for g in range(8):
                last = pe.matmul(acc[:, g // 2, (g % 2) * SEQ:(g % 2 + 1) * SEQ], a_bd[:, g, :],
                                 a_xc[:, g % 4, :], start=True, stop=True)
            last.then_inc(*sig("gates", l))
            for j in (2, 3, 4):
                turn(j)
            pe.wait_ge(*when("gate_sig", l))
            for j in range(2):
                rows(pe, c + 6 + j, lambda t, nn: acc[:, t, j * SEQ:(j + 1) * SEQ],
                     lambda kt: xT[:, kt, :, :], KT, 1, True, True, view=half)
                if j == 0:
                    turn(5)
            pe.wait_ge(*when("turned", ("a", l, 5)))
            pe.wait_ge(*when("v_out", ("a", l)))

            def outer_gate():
                for j in (8, 9):
                    yield from columns_by_steps(pe, c + j, lambda f: a_bank(j)[:, f * SEQ:(f + 1) * SEQ], 2, KT, SEQ)

            feed = outer_gate()
            if l == 0:
                pe.wait_ge(*when("masks", 0))
            for s in range(8 + 4):
                if s < 8:
                    if s >= 2:
                        pe.wait_ge(*when("exps", ("a", l, s - 2)))
                    hd, comp = s // 2, s % 2
                    r = slice(HD * comp, HD * comp + HD)
                    score_map(pe, s % 2, a_q[r, hd, :], a_k[r, hd, :], ("a", l, s))
                    for _ in range(A_UNITS):
                        next(feed, None)
                if s % 2 == 0 and 2 <= s <= 8:
                    hd = s // 2 - 1
                    pe.wait_ge(*when("weights", ("a", l, hd)))
                    map_transpose(pe, 2 + hd % 2, probs[:, 2 * (hd % 2) + 1, :], ("a", l, hd))
                if s % 2 == 0 and s >= 4:
                    hd = s // 2 - 2
                    if hd >= 4:
                        continue
                    pe.wait_ge(*when("flip_out", ("a", l, hd)))
                    w = att_T[:, 0:CAUSAL]
                    o = [acc[:, 2 + t, hd * P:(hd + 1) * P] for t in range(TT)]
                    v = [a_v[:, t, hd * P:(hd + 1) * P] for t in range(TT)]
                    pe.matmul(o[0], w[:, 0:P], v[0], start=True, stop=True)
                    pe.matmul(o[1], w[:, P:2 * P], v[0], start=True, stop=False)
                    pe.matmul(o[1], w[:, 2 * P:3 * P], v[1], start=False, stop=True).then_inc(*sig("head_out", ("a", l, hd)))
            def flip_heads():
                pe.wait_ge(*when("o_normed", l))
                for j in range(4):
                    for t in range(TT):
                        last = pe.transpose(tb[:, j // 2, (j % 2) * SEQ + t * P:(j % 2) * SEQ + (t + 1) * P],
                                            a_o[:, t, j * P:(j + 1) * P], ident)
                last.then_inc(*sig("o_T", l))

            pe.wait_ge(*when("y_lo", l))
            pe.wait_ge(*when("own", ("oc", l)))
            for j in range(4):
                if j >= 2:
                    pe.wait_ge(*when("cat_lo", ("a", l, j - 2)))
                rows(pe, c + 10 + j, acc_tn, lambda kt: cat[:, 2 * ((j + 2) % 4) + kt, :, :], 2, 2, j == 0, j == 3, view=wide,
                     acc_done=c + 13 if j == 3 else None,
                     before_last=flip_lower(pe, n) if j == 3 else flip_heads if j == 1 else None)

        def mix_a_act(act, l, c, n):
            for j in range(6):
                split_hi(act, c, j + SPLIT)
            act.wait_ge(*when("gates", l))
            for t in range(4):
                act.activation(a_r[:, t, :], acc[:, t // 2, (t % 2) * SEQ:(t % 2 + 1) * SEQ], ACT.Sigmoid,
                               bias=lru_par[:, l, L_BA + t:L_BA + t + 1]).then_inc(*sig("own_act", ("r", l, t)))
            for t in range(4):
                last = act.activation(a_i[:, t, :], acc[:, 2 + t // 2, (t % 2) * SEQ:(t % 2 + 1) * SEQ], ACT.Sigmoid,
                                      bias=lru_par[:, l, L_BX + t:L_BX + t + 1])
            last.then_inc(*sig("gate_sig", l))
            act.wait_ge(*when("own_act", ("r", l, 3)))
            for t in range(4):
                act.activation(a_a[:, t, :], a_r[:, t, :], ACT.Exp, scale=sp8n[:, 4 * l + t:4 * l + t + 1])
                last = act.activation(a_th[:, t, :], a_r[:, t, :], ACT.Tanh, scale=sp8[:, 4 * l + t:4 * l + t + 1])
            last.then_inc(*sig("decay", l))
            split_hi(act, c, 6 + SPLIT)
            act.wait_ge(*when("lru_m", l))
            act.activation(a_th[:, :, :], a_th[:, :, :], ACT.Sqrt).then_inc(*sig("lru_root", l))
            used(act, c + 7)
            for t in range(TT):
                last = act.activation(a_v[:, t, :], acc[:, t, :], ACT.Copy, scale=rstd[:, t:t + 1])
            last.then_inc(*sig("v_out", ("a", l)))
            split_hi(act, c, 7 + SPLIT)
            for s in range(9):
                if s < 8:
                    if s >= 4:
                        act.wait_ge(*when("flipped", ("a", l, s // 2 - 2)))
                    map_exp(act, s, s % 2, probs[:, s % 4, :], ("a", l, s), HD ** -0.5)
                if s % 2 == 0 and s >= 2:
                    hd = s // 2 - 1
                    act.wait_ge(*when("flipped", ("a", l, hd)))
                    if hd:
                        act.wait_ge(*when("head_out", ("a", l, hd - 1)))
                    act.activation(att_T[:, 0:CAUSAL], tb[:, 2 + hd % 2, 0:CAUSAL], ACT.Copy).then_inc(*sig("flip_out", ("a", l, hd)))
                if s in (3, 6):
                    split_hi(act, c, 7 + s // 3 + SPLIT)
                if s == 7:
                    act.wait_ge(*when("a_taken", (l, 9)))
                    act.activation(a_gr[:, :, :], a_gr[:, :, :], ACT.Gelu_apprx_tanh).then_inc(*sig("lru_gelu", l))
            act.wait_ge(*when("lru_y", l))
            act.activation(cat[:, 4:8, 0, :], a_gr[:, :, :], ACT.Copy).then_inc(*sig("y_hi", l))
            act.wait_ge(*when("o_ms", l))
            act.activation(s8[1], s8[0], ACT.Sqrt).then_inc(*sig("root", ("a", l)))
            split_hi(act, c, 10 + SPLIT)
            for b in range(2):
                if b == 0:
                    act.wait_ge(*when("o_T", l))
                act.activation(cat[:, 2 * b:2 * b + 2, 0, :], two(tb[:, b, :]), ACT.Copy).then_inc(*sig("cat_hi", ("a", l, b)))
            for j in range(11, 13):
                split_hi(act, c, j + SPLIT)

        def mix_a_dve(dve, l, c, n):
            def take(j):
                used(dve, c + j)
                by_rb(dve, a_dst(j), two(a_bank(j)), n, j == 0).then_inc(*sig("a_taken", (l, j)))
                if j < 9:
                    split_lo(dve, c, j + SPLIT)

            def turn(j):
                b, bank = a_qk(j)
                r = two(xn[:, 1, 512 * (j % 2):512 * (j % 2) + 512])
                dve.wait_ge(*when("rotated", ("a", l, j)))
                if j >= 4:
                    dve.wait_ge(*when("turned", ("a", l, j - 2)))
                dve.tensor_tensor(r, two(bank), ropeA[:, 1, :].unsqueeze(1).to_broadcast([P, 2, SEQ]), ALU.mult)
                dve.tensor_tensor(b, b, ropeA[:, 0, :].unsqueeze(1).to_broadcast([P, 2, SEQ]),
                                  ALU.mult).then_inc(*sig("own", ("turn", "a", l, j)))
                dve.wait_ge(*when("own", ("turn", "a", l, j)))
                dve.tensor_tensor(b, b, r, ALU.add).then_inc(*sig("turned", ("a", l, j)))

            for j in range(2):
                take(j)
            par = lru_par[:, l, :]
            for t in range(4):
                if t % 2 == 0:
                    dve.wait_ge(*when("a_taken", (l, t // 2)))
                for k_ in range(4):
                    src = a_x[:, t, k_:k_ + SEQ]
                    w = par[:, L_CONV + 4 * k_ + t:L_CONV + 4 * k_ + t + 1]
                    if k_ == 0:
                        ins = dve.tensor_scalar(a_xc[:, t, :], src, w, par[:, L_CONVB + t:L_CONVB + t + 1], ALU.mult, ALU.add)
                    else:
                        dve.wait_ge(*when("own", ("cv", l, t, k_ - 1)))
                        ins = dve.scalar_tensor_tensor(a_xc[:, t, :], src, w, a_xc[:, t, :], ALU.mult, ALU.add)
                    ins.then_inc(*(sig("conv", (l, t)) if k_ == 3 else sig("own", ("cv", l, t, k_))))
            for j in range(2, 6):
                take(j)
            for j in (2, 3, 4):
                turn(j)
            dve.wait_ge(*when("decay", l))
            dve.tensor_tensor(a_r[:, :, :], a_a[:, :, :], a_a[:, :, :], ALU.mult).then_inc(*sig("own", ("aa", l)))
            dve.wait_ge(*when("own", ("aa", l)))
            dve.scalar_tensor_tensor(a_th[:, :, :], a_r[:, :, :], 1.0, a_th[:, :, :], ALU.add, ALU.mult).then_inc(*sig("lru_m", l))
            split_lo(dve, c, 6 + SPLIT)
            turn(5)
            dve.tensor_tensor(a_i[:, :, :], a_i[:, :, :], a_xc[:, :, :], ALU.mult).then_inc(*sig("own", ("ix", l)))
            split_lo(dve, c, 7 + SPLIT)
            dve.wait_ge(*when("lru_root", l))
            dve.wait_ge(*when("own", ("ix", l)))
            dve.tensor_tensor(a_i[:, :, :], a_i[:, :, :], a_th[:, :, :], ALU.mult).then_inc(*sig("own", ("b", l)))
            dve.wait_ge(*when("own", ("b", l)))

            def scan(t):
                dve.tensor_tensor_scan(a_xc[:, t, :], a_a[:, t, :], a_i[:, t, :], 0.0, ALU.mult, ALU.add).then_inc(*sig("own", ("scan", l, t)))

            for s in range(9):
                if s < 8:
                    map_stats(dve, s, s % 2, ("a", l, s), HD ** -0.5)
                if s >= 1:
                    m = s - 1
                    pr = probs[:, m % 4, :]
                    dve.wait_ge(*when("exps", ("a", l, m)))
                    dve.reciprocal(rs[:, m, :], sm[:, m, :]).then_inc(*sig("own", ("rs", "a", l, m)))
                    dve.wait_ge(*when("own", ("rs", "a", l, m)))
                    if m % 2 == 0:
                        dve.tensor_scalar(pr[:, 0:P], pr[:, 0:P], rs[:, m, 0:1], None, ALU.mult)
                        dve.tensor_scalar(pr[:, P:CAUSAL], pr[:, P:CAUSAL], rs[:, m, 1:2], None,
                                          ALU.mult).then_inc(*sig("own", ("p0", "a", l, m)))
                    else:
                        dve.tensor_scalar(cf, rs[:, m, :], lam[:, l:l + 1], -1.0, ALU.mult, ALU.mult).then_inc(*sig("own", ("cf", l, m)))
                        dve.wait_ge(*when("own", ("cf", l, m)))
                        dve.wait_ge(*when("own", ("p0", "a", l, m - 1)))
                        first = probs[:, (m - 1) % 4, :]
                        dve.scalar_tensor_tensor(pr[:, 0:P], pr[:, 0:P], cf[:, 0:1], first[:, 0:P], ALU.mult, ALU.add)
                        dve.scalar_tensor_tensor(pr[:, P:CAUSAL], pr[:, P:CAUSAL], cf[:, 1:2], first[:, P:CAUSAL],
                                                 ALU.mult, ALU.add).then_inc(*sig("weights", ("a", l, m // 2)))
                        dve.wait_ge(*when("weights", ("a", l, m // 2)))
                if s in (3, 6):
                    take(7 + s // 3)
                elif s in (2, 4, 5, 7):
                    scan((2, 4, 5, 7).index(s))
            dve.wait_ge(*when("lru_gelu", l))
            dve.wait_ge(*when("own", ("scan", l, 3)))
            dve.tensor_tensor(a_gr[:, :, :], a_gr[:, :, :], a_xc[:, :, :], ALU.mult).then_inc(*sig("lru_y", l))
            dve.wait_ge(*when("y_hi", l))
            dve.tensor_tensor(cat[:, 4:8, 1, :], a_gr[:, :, :], cat[:, 4:8, 0, :], ALU.subtract).then_inc(*sig("y_lo", l))
            dve.wait_ge(*when("head_out", ("a", l, 3)))
            dve.tensor_copy(a_o[:, :, :], acc[:, 2:4, :]).then_inc(*sig("own", ("oc", l)))
            dve.wait_ge(*when("own", ("oc", l)))
            o2 = cut(5120, TT, 512)
            dve.tensor_tensor(o2, a_o[:, :, :], a_o[:, :, :], ALU.mult).then_inc(*sig("own", ("osq", l)))
            dve.wait_ge(*when("own", ("osq", l)))
            dve.tensor_reduce(s8[2], cut(5120, 8, P), AX.X, ALU.add).then_inc(*sig("own", ("oss", l)))
            dve.wait_ge(*when("own", ("oss", l)))
            dve.tensor_scalar(s8[0], s8[2], 1.0 / P, EPS, ALU.mult, ALU.add).then_inc(*sig("o_ms", l))
            newton(dve, s8[1], s8[0], s8[3], s8[4], s8[5], ("a", l))
            for t in range(TT):
                for hd in range(4):
                    o = a_o[:, t, hd * P:(hd + 1) * P]
                    last = dve.scalar_tensor_tensor(o, o, s8[5][:, 4 * t + hd:4 * t + hd + 1], gsub[:, l, :], ALU.mult, ALU.mult)
            last.then_inc(*sig("o_normed", l))
            split_lo(dve, c, 9 + SPLIT)
            split_lo(dve, c, 10 + SPLIT)
            for b in range(2):
                dve.wait_ge(*when("cat_hi", ("a", l, b)))
                dve.tensor_tensor(cat[:, 2 * b:2 * b + 2, 1, :], two(tb[:, b, :]), cat[:, 2 * b:2 * b + 2, 0, :],
                                  ALU.subtract).then_inc(*sig("cat_lo", ("a", l, b)))
            split_lo(dve, c, 11 + SPLIT)
            residual(dve, n, c + 13)

        def start_act(act):
            act.wait_ge(*when("dots", 0))
            act.activation(dexp, dots, ACT.Exp).then_inc(*sig("dexp", 0))
            act.wait_ge(*when("lam_abs", 0))
            act.activation(t8b, t8a, ACT.Exp, scale=-1.0).then_inc(*sig("own_act", "st0"))
            act.wait_ge(*when("own_act", "st0"))
            act.activation(t8b, t8b, ACT.Ln, bias=1.0).then_inc(*sig("lam_ln", 0))
            act.wait_ge(*when("angle", 0))
            act.activation(ropeA[:, 1, :], cut(1024, SEQ), ACT.Sin)
            act.activation(ropeA[:, 0, :], cut(1536, SEQ), ACT.Sin).then_inc(*sig("sines", 0))

        def start_dve(dve):
            steps = [0]

            def own(ins):
                steps[0] += 1
                ins.then_inc(*sig("own", ("start", steps[0])))
                dve.wait_ge(*when("own", ("start", steps[0])))

            dve.wait_ge(*when("start_in", 3))
            prod = cut(512, 256)
            own(dve.tensor_tensor(prod, cut(0, 256), cut(256, 256), ALU.mult))
            dve.tensor_reduce(dots, prod.rearrange("p (a d) -> p a d", a=4), AX.X, ALU.add).then_inc(*sig("dots", 0))
            dve.scalar_tensor_tensor(t8a.rearrange("p (l t) -> p l t", l=2), lru_par[:, :, L_LAM:L_END], -1.0,
                                     lru_par[:, :, L_LAM:L_END], ALU.mult, ALU.max).then_inc(*sig("lam_abs", 0))
            dve.wait_ge(*when("dexp", 0))
            for l in range(DEPTH_A):
                init = 0.8 - 0.6 * math.exp(-0.3 * l)
                own(dve.tensor_tensor(lam[:, l:l + 1], dexp[:, 2 * l:2 * l + 1], dexp[:, 2 * l + 1:2 * l + 2], ALU.subtract))
                own(dve.tensor_scalar(lam[:, l:l + 1], lam[:, l:l + 1], init, None, ALU.add))
                own(dve.tensor_scalar(gsub[:, l, :], gsub[:, l, :], 1.0 - init, None, ALU.mult))
            own(dve.tensor_scalar(sp8.rearrange("p (l t) -> p l t", l=2), lru_par[:, :, L_LAM:L_END], -1.0, 0.0, ALU.mult, ALU.max))
            dve.wait_ge(*when("lam_ln", 0))
            own(dve.tensor_tensor(sp8, sp8, t8b, ALU.add))
            own(dve.tensor_scalar(sp8, sp8, 8.0, None, ALU.mult))
            own(dve.tensor_scalar(sp8n, sp8, -1.0, None, ALU.mult))
            ang, turns, angc, tmp = cut(1024, SEQ), cut(1280, SEQ), cut(1536, SEQ), cut(1792, SEQ)
            own(dve.tensor_copy(ang, ropeA[:, 1, :].bitcast(mybir.dt.int32)))
            own(dve.tensor_scalar(ang, ang, cst[:, C_FREQ:C_FREQ + 1], None, ALU.mult))
            magic = 1.5 * 2.0 ** 23
            own(dve.tensor_scalar(turns, ang, 1.0 / (2 * math.pi), magic, ALU.mult, ALU.add))
            own(dve.tensor_scalar(turns, turns, magic, None, ALU.subtract))
            p1 = 6.28125
            p2 = float(np.float32(round((2 * math.pi - p1) * 2 ** 20) / 2 ** 20))
            p3 = 2 * math.pi - p1 - p2
            for part in (p1, p2, p3):
                own(dve.scalar_tensor_tensor(ang, turns, -part, ang, ALU.mult, ALU.add))
            own(dve.tensor_scalar(ang, ang, 3.1415925, -3.1415925, ALU.min, ALU.max))
            own(dve.scalar_tensor_tensor(tmp, ang, -1.0, ang, ALU.mult, ALU.max))
            dve.tensor_scalar(angc, tmp, -1.0, math.pi / 2, ALU.mult, ALU.add).then_inc(*sig("angle", 0))
            dve.wait_ge(*when("sines", 0))

        MIX = {"mix_a": (mix_a_pe, mix_a_act, mix_a_dve), "mlp": (mlp_pe, mlp_act, mlp_dve),
               "ple": (ple_pe, ple_act, ple_dve), "ffn": (ffn_pe, ffn_act, ffn_dve),
               "stick": (stick_pe, stick_act, stick_dve), "moba": (moba_pe, moba_act, moba_dve),
               "mla": (mla_pe, mla_act, mla_dve)}

        raw_full = [S.sem(f"raw_full{s}") for s in range(RAW)]
        hi_done, lo_done, chunk_used = S.sem("hi_done"), S.sem("lo_done"), S.sem("chunk_used")
        hid_t, hid_u, hid_v, hid_g, hid_hi, hid_lo = [S.sem(n_) for n_ in ("hid_t", "hid_u", "hid_v", "hid_g", "hid_hi", "hid_lo")]
        block = ctx.enter_context(nc.Block())

        @block.sync
        def _(sp):
            xv = x.rearrange("(t p) d -> p t d", p=P)
            for t in range(TT):
                sp.dma_start(h[:, t, :], xv[:, t, :]).then_inc(*sig(f"x_in{t}", 0, 16))

            def load(k, row):
                sp.dma_start(raw[:, k, :], stream[row, :, :]).then_inc(raw_full[k], 16)

            for k in range(RAW):
                load(k, k)
            with sp.Fori(0, N_CHUNKS // RAW - 1) as i:
                for k in range(RAW):
                    sp.wait_ge(lo_done, k + 1 + RAW * i)
                    load(k, i * RAW + (RAW + k))
            for t in range(TT):
                sp.wait_ge(*when("normed", (N_NORMS - 1, t)))
                sp.dma_start(out[t * P:(t + 1) * P, :], xn[:, t, :]).then_inc(*sig("stored", t, 16))
            sp.wait_ge(*when("stored", TT - 1))

        @block.gpsimd
        def _(pool):
            pool.memset(zero[:, :], 0.0).then_inc(*sig("zeroed", 0))
            pool.memset(a_x[:, :, 0:3], 0.0).then_inc(*sig("zeroed", "x"))
            pool.dma_start(lru_par[:, :, :], lru_cols).then_inc(*sig("start_in", 0, 16))
            pool.dma_start(ropeA[:, 1, :].bitcast(mybir.dt.int32), positions.partition_broadcast(P)).then_inc(*sig("start_in", 1, 16))
            pool.dma_start(gsub[:, :, :], g_subln.partition_broadcast(P)).then_inc(*sig("start_in", 2, 16))
            pool.dma_start(cut(0, 512), lam_qk.partition_broadcast(P)).then_inc(*sig("start_in", 3, 16))
            pool.dma_start(gain[:, :], gains[0, :].partition_broadcast(P)).then_inc(*sig("gain_in", BRIDGE, 16))
            for kind, l, c, n in PHASES:
                if kind == "mix_a":
                    pool.wait_ge(*when("sumsq", (n, 1)))
                    pool.dma_start(a_bd, gates[l, :, :]).then_inc(*sig("gates_in", l, 16))
                if kind == "ple":
                    pool.wait_ge(*when("h_new", (n - 1, 1, 1)))
                    pool.dma_start(p_in, pT[l, :, :, :]).then_inc(*sig("p_in", l, 16))
                if kind == "bridge":
                    pool.wait_ge(*when("normed", (n, 1)))
                    pool.dma_start(gain[:, 0:MLA_QR + MLA_KVR], gains[2, 0:MLA_QR + MLA_KVR].partition_broadcast(P))\
                        .then_inc(*sig("gain_in", "mla", 16))
                if kind == "mla":
                    pool.wait_ge(*when("lat_normed", (l, 1)))
                    pool.dma_start(gain[:, :], gains[1, :].partition_broadcast(P)).then_inc(*sig("gain_in", N_NORMS - 1, 16))

        @block.tensor
        def _(pe):
            last_kind = None
            pe.wait_ge(*when("ident_in", 0))
            for kind, l, c, n in PHASES[:-1]:
                if kind != "bridge":
                    norm_pe(pe, n, last_kind)
                    MIX[kind][0](pe, l, c, n)
                last_kind = kind

        @block.scalar
        def _(act):
            act.dma_start(cst[:, 0:P], consts[:, 0:P]).then_inc(*sig("ident_in", 0, 16))
            act.dma_start(gain_T[:, :, :], gains_T).then_inc(*sig("gain_T_in", 0, 16))
            act.dma_start(cst[:, P:C_END], consts[:, P:C_END]).then_inc(*sig("const_in", 0, 16))
            act.wait_ge(*when("gain_T_in", 0))
            last_kind = None
            for kind, l, c, n in PHASES:
                if kind not in ("bridge", "end"):
                    norm_act(act, n)
                if n == 0:
                    for k in range(SPLIT):
                        split_hi(act, k)
                elif kind != "bridge":
                    split_hi(act, c, -1 + SPLIT)
                factor_act(act, n)
                if n == 0:
                    start_act(act)
                spread_act(act, n, kind)
                if kind not in ("bridge", "end"):
                    MIX[kind][1](act, l, c, n)
                last_kind = kind

        @block.vector
        def _(dve):
            dve.wait_ge(*when("x_in0", 0))
            for t in range(TT):
                dve.wait_ge(*when(f"x_in{t}", 0))
                for half_ in range(2):
                    dve.nop().then_inc(*sig("h_new", (0, t, half_)))
            last_kind = None
            for kind, l, c, n in PHASES:
                if kind not in ("bridge", "end"):
                    norm_dve(dve, n, last_kind)
                if n == 0:
                    for k in range(SPLIT):
                        split_lo(dve, k)
                    dve.wait_ge(*when("const_in", 0))
                    dve.tensor_copy(bfc[:, 0, :], ident)
                    dve.tensor_copy(bfc[:, 1, :], cst[:, C_CAUSNEG:C_CAUSNEG + P])
                    dve.tensor_copy(bfc[:, 2, :], cst[:, C_STRNEG:C_STRNEG + P]).then_inc(*sig("masks", 0))
                else:
                    if last_kind != "bridge":
                        split_lo(dve, c, -2 + SPLIT)
                    if kind not in ("bridge", "mlp"):
                        split_lo(dve, c, -1 + SPLIT)
                factor_dve(dve, n, kind)
                if kind == "mlp":
                    split_lo(dve, c, -1 + SPLIT)
                if n == 0:
                    start_dve(dve)
                if kind == "mix_a":
                    dve.wait_ge(*when("zeroed", "x"))
                if kind not in ("bridge", "end"):
                    MIX[kind][2](dve, l, c, n)
                last_kind = kind
    return S.marks


def write_program(new, declare):
    nc = new()
    known = write(nc, None, *declare(nc))
    nc = new()
    write(nc, known, *declare(nc))
    return nc


def constants():
    c = np.zeros((P, C_END), np.float32)
    k, m = np.arange(P)[:, None], np.arange(P)[None, :]
    c[:, C_ID:C_ID + P] = k == m
    for at, heads, first, half_ in ((C_ROT, (0, HD), 0, HD // 8), (C_ROTL, (0,), HD, MLA_ROPE // 2)):
        for h0 in heads:
            for j in range(half_):
                a = h0 + first + j
                c[a + half_, at + a] = -1.0
                c[a, at + a + half_] = 1.0
    c[:, C_TRI:C_TRI + P] = -8.0 * (k >= m)
    c[:, C_ALL:C_ALL + P] = -8.0
    c[:, C_STRICT:C_STRICT + P] = k < m
    c[:, C_CAUSNEG:C_CAUSNEG + P] = NEG * (m > k)
    c[:, C_STRNEG:C_STRNEG + P] = NEG * (k >= m)
    pos = np.arange(SEQ, dtype=np.float32)
    for cos_at, sin_at, r, firsts in ((C_COSM, C_SINM, HD // 4, (0, HD)), (C_COSL, C_SINL, MLA_ROPE, (HD,))):
        inv = np.float32(THETA) ** (-np.arange(0, r, 2, dtype=np.float32) / np.float32(r))
        ang = pos[None, :] * inv[:, None]
        c[:, cos_at:cos_at + SEQ] = 1.0
        for f in firsts:
            for half_ in range(2):
                rows_ = slice(f + half_ * (r // 2), f + (half_ + 1) * (r // 2))
                c[rows_, cos_at:cos_at + SEQ] = np.cos(ang)
                c[rows_, sin_at:sin_at + SEQ] = np.sin(ang)
                if r == HD // 4:
                    c[rows_, C_FREQ] = inv
    return c


def column_chunks(w, width=SEQ):
    kt = w.shape[0] // P
    v = w.reshape(kt, P, w.shape[1] // width, width)
    return list(v.transpose(2, 1, 0, 3).reshape(w.shape[1] // width, P, kt * width))


def row_chunks(w):
    return list(w.reshape(w.shape[0] // (2 * P), 2, P, D).transpose(0, 2, 1, 3).reshape(-1, P, 2 * D))


def lay_stream(a):
    out = []

    def woven(ups, downs):
        out.extend(u[0] for u in ups)
        for k in range(1, len(downs)):
            out.extend(u[k] for u in ups)
            out.append(downs[k - 1])
        out.append(downs[-1])

    for l in range(DEPTH_A):
        w = a["w_in"][l]
        q, k, v, xr, gr = (w[:, 512 * j:512 * (j + 1)] for j in range(5))
        for part in (xr, q, k, v, gr):
            out.extend(column_chunks(part))
        w_out = row_chunks(a["w_out"][l])
        out.extend(w_out[2:] + w_out[:2])
        woven([column_chunks(a["w_mlp_in"][l])], row_chunks(a["w_mlp_out"][l]))
        out.extend(row_chunks(a["w_ple_gate"][l]))
        out.extend(row_chunks(a["w_ple_proj"][l]))

    def swiglu(f, i):
        gu = a[f + "_w_gate_up_2"][i]
        woven([column_chunks(gu[:, :D_FF_B]), column_chunks(gu[:, D_FF_B:])], row_chunks(a[f + "_w_down_2"][i]))

    for i in range(DEPTH_B):
        swiglu("ffn1", i)
        kind = MIXERS[i]
        if kind == "mla":
            w = a["mla_w_in_2"][0]
            for at in (0, SEQ, MLA_IN - SEQ):
                out.extend(column_chunks(w[:, at:at + SEQ]))
            at = 0
            for heads in MLA_Q_GROUPS:
                n = heads * MLA_HD
                part = a["mla_w_uq_2"][0][:, at:at + n].reshape(3, P, n).transpose(1, 0, 2).reshape(P, 3 * n)
                out.append(np.pad(part, ((0, 0), (0, CH - 3 * n))))
                at += n
            for g in range(2):
                out.extend(row_chunks(a["mla_w_ukv_2"][0][:, g * D:(g + 1) * D]))
            out.extend(row_chunks(a["mla_w_o_2"][0]))
        else:
            w = a["sb_w_qkv_2"][i // 3] if kind == "stick" else a["moba_w_qkv_2"][0]
            o = a["sb_w_o_2"][i // 3] if kind == "stick" else a["moba_w_o_2"][0]
            q, k, v = (column_chunks(w[:, at:at + D]) for at in (0, D, 2 * D))
            out.extend(v)
            for pair in zip(q, k):
                out.extend(pair)
            out.extend(row_chunks(o))
        swiglu("ffn2", i)
    assert len(out) == N_CHUNKS, len(out)
    return np.stack(out)


def lay_out(a):
    gains = []
    for l in range(DEPTH_A):
        gains += [a["g_mix"][l], a["g_mlp"][l], a["g_ple"][l]]
    gains.append(a["g_final"])
    for i in range(DEPTH_B):
        gains += [a["norm_ffn1_2"][i], a["norm_mix_2"][i], a["norm_ffn2_2"][i]]
    gains.append(a["final_norm_2"])
    mla = np.zeros((D,), np.float32)
    mla[:MLA_QR + MLA_KVR] = np.concatenate([a["mla_q_norm_2"][0], a["mla_kv_norm_2"][0]])
    lru, gates = [], []
    for l in range(DEPTH_A):
        r = [a["conv_w"][l].reshape(16, P)] + [a[n][l].reshape(4, P) for n in ("conv_b", "b_gate_a", "b_gate_x", "lru_lambda")]
        lru.append(np.concatenate(r))
        bd = np.zeros((P, 8, P), np.float32)
        for m, name in enumerate(("w_gate_a", "w_gate_x")):
            for g in range(8):
                o = HD * (g % 2)
                bd[o:o + HD, 4 * m + g // 2, o:o + HD] = a[name][l][g]
        gates.append(bd.reshape(P, 8 * P))
    p = a["p"][:, 0]
    return {
        "stream": lay_stream(a),
        "x": a["x"][0],
        "pT": np.ascontiguousarray(p.transpose(0, 2, 1).reshape(DEPTH_A, 2, P, SEQ).transpose(0, 2, 1, 3)),
        "positions": a["positions"][0],
        "gains": np.stack([gains[BRIDGE], gains[N_NORMS - 1], mla]),
        "gains_T": np.ascontiguousarray(np.stack(gains).reshape(N_NORMS, KT, P).transpose(2, 0, 1)),
        "g_subln": a["g_subln"],
        "lam_qk": np.concatenate([a["lam_q"].reshape(-1), a["lam_k"].reshape(-1)]),
        "lru_cols": np.ascontiguousarray(np.stack(lru).transpose(2, 0, 1)),
        "gates": np.stack(gates),
        "consts": constants(),
    }


def kernel(**inputs):
    import concourse.bacc as bacc
    from concourse.bass_utils import run_bass_kernel_spmd as run

    arrays = lay_out({k: np.asarray(v) for k, v in inputs.items()})

    def new():
        return bacc.Bacc("TRN2", target_bir_lowering=False, num_devices=1)

    def declare(nc):
        aps = [nc.dram_tensor("in_" + k, v.shape, mybir.dt.from_np(v.dtype), kind="ExternalInput").ap()
               for k, v in arrays.items()]
        return aps + [nc.dram_tensor("out", (SEQ, D), mybir.dt.float32, kind="ExternalOutput").ap()]

    nc = write_program(new, declare)
    r = run(nc, [{"in_" + k: v for k, v in arrays.items()}], core_ids=[0])
    return r.results[0]["out"].reshape(1, SEQ, D)
```
